# Optimizing a Trainium2 kernel written in Bass

```python
import math
import jax
import jax.numpy as jnp
from jax import lax
import numpy as np

D_MODEL = 1024
BATCH = 1
SEQ = 256
DEPTH = 1

CHUNK = 64
MEM_LEN = 256
EPS = 1e-6
CONV_WIDTH = 4

LRU_WIDTH = 1024
LRU_HEADS = 8
LRU_HEAD_DIM = LRU_WIDTH // LRU_HEADS
LRU_C = 8.0

SGU_WIDTH = 1024
SGU_GROUPS = 4
SGU_GROUP_DIM = SGU_WIDTH // SGU_GROUPS
SGU_BLOCK = 128

SSM_WIDTH = 1024
SSM_HEAD_DIM = 64
SSM_HEADS = SSM_WIDTH // SSM_HEAD_DIM
SSM_GROUPS = 4
SSM_HEADS_PER_GROUP = SSM_HEADS // SSM_GROUPS
SSM_STATE = 128
SSM_CHUNK = CHUNK
SSM_CONV_DIM = SSM_WIDTH + 2 * SSM_GROUPS * SSM_STATE

N_BRANCHES = 3

OFF_YA = LRU_WIDTH
OFF_UV = 2 * LRU_WIDTH
OFF_Z = OFF_UV + 2 * SGU_WIDTH
OFF_XBC = OFF_Z + SSM_WIDTH
OFF_DT = OFF_XBC + SSM_CONV_DIM
OFF_GATE = OFF_DT + SSM_HEADS
IN_DIM = OFF_GATE + N_BRANCHES * D_MODEL

XA_HEADS = 4
XA_HEAD_DIM = D_MODEL // XA_HEADS

N_EXPERT_GROUPS = 4
EXPERTS_PER_GROUP = 8
N_EXPERTS = N_EXPERT_GROUPS * EXPERTS_PER_GROUP
TOP_K_IN_GROUP = 2
D_EXPERT = 512
MOE_BLOCK = 256

kernel_name = 'hybrid_rglru_gmlp_ssd_hmoe_encoder'

def rmsnorm(x, g):
    xf = x.astype(jnp.float32)
    y = xf * lax.rsqrt(jnp.mean(xf * xf, axis=-1, keepdims=True) + EPS)
    return (y * g.astype(jnp.float32)).astype(x.dtype)

def layernorm(x, g):
    xf = x.astype(jnp.float32)
    xc = xf - jnp.mean(xf, axis=-1, keepdims=True)
    y = xc * lax.rsqrt(jnp.mean(xc * xc, axis=-1, keepdims=True) + EPS)
    return (y * g.astype(jnp.float32)).astype(x.dtype)

def causal_depthwise_conv(x, w, b):
    k = w.shape[0]
    y = lax.conv_general_dilated(
        x, w[:, None, :].astype(x.dtype), window_strides=(1,),
        padding=[(k - 1, 0)], dimension_numbers=('NWC', 'WIO', 'NWC'),
        feature_group_count=x.shape[-1])
    return y + b.astype(x.dtype)

def rglru_branch(xa, ya, conv_w, conv_b, gx_w, gx_b, ga_w, ga_b, lam):
    bsz, s, _ = xa.shape
    xc = causal_depthwise_conv(xa, conv_w, conv_b)
    xh = xc.reshape(bsz, s, LRU_HEADS, LRU_HEAD_DIM)
    gate_x = jax.nn.sigmoid(jnp.einsum('bshi,hij->bshj', xh, gx_w) + gx_b).reshape(bsz, s, LRU_WIDTH)
    gate_a = jax.nn.sigmoid(jnp.einsum('bshi,hij->bshj', xh, ga_w) + ga_b).reshape(bsz, s, LRU_WIDTH)
    log_a = (-LRU_C * gate_a.astype(jnp.float32)) * jax.nn.softplus(-lam.astype(jnp.float32))
    a = jnp.exp(log_a)
    mult = jnp.sqrt(jnp.maximum(1.0 - jnp.exp(2.0 * log_a), 0.0))
    b = xc.astype(jnp.float32) * gate_x.astype(jnp.float32) * mult

    def combine(left, right):
        return left[0] * right[0], right[0] * left[1] + right[1]

    _, h = lax.associative_scan(combine, (a, b), axis=1)
    return h.astype(xa.dtype) * jax.nn.gelu(ya)

def sgu_branch(uv, norm_g, w_s, b_s):
    z = jax.nn.gelu(uv)
    u, v = jnp.split(z, 2, axis=-1)
    v = layernorm(v, norm_g)
    bsz, s, _ = v.shape
    nb = s // SGU_BLOCK
    vb = v.reshape(bsz, nb, SGU_BLOCK, SGU_GROUPS, SGU_GROUP_DIM)
    chunk_id = jnp.arange(SGU_BLOCK) // CHUNK
    mask = chunk_id[None, :] <= chunk_id[:, None]
    w = jnp.where(mask[None], w_s, 0.0).astype(v.dtype)
    mixed = jnp.einsum('gts,bnsgd->bntgd', w, vb) + b_s.T.astype(v.dtype)[None, None, :, :, None]
    return u * mixed.reshape(bsz, s, SGU_WIDTH)

def ssd_branch(z, xbc, dt, conv_w, conv_b, dt_bias, a_log, d_skip, norm_g):
    bsz, s, _ = z.shape
    g_, r_, p_, n_, l_ = SSM_GROUPS, SSM_HEADS_PER_GROUP, SSM_HEAD_DIM, SSM_STATE, SSM_CHUNK
    nc = s // l_
    xbc = jax.nn.silu(causal_depthwise_conv(xbc, conv_w, conv_b))
    xs, bm, cm = jnp.split(xbc, [SSM_WIDTH, SSM_WIDTH + g_ * n_], axis=-1)
    x = xs.reshape(bsz, nc, l_, g_, r_, p_).astype(jnp.float32)
    bm = bm.reshape(bsz, nc, l_, g_, n_).astype(jnp.float32)
    cm = cm.reshape(bsz, nc, l_, g_, n_).astype(jnp.float32)
    dt = jax.nn.softplus(dt.astype(jnp.float32) + dt_bias.astype(jnp.float32)).reshape(bsz, nc, l_, g_, r_)
    a = -jnp.exp(a_log.astype(jnp.float32)).reshape(g_, r_)
    cs = jnp.cumsum(dt * a, axis=2)
    seg = cs[:, :, :, None] - cs[:, :, None, :]
    causal = (jnp.arange(l_)[:, None] >= jnp.arange(l_)[None, :])[None, None, :, :, None, None]
    decay = jnp.exp(jnp.where(causal, seg, -jnp.inf))
    cb = jnp.einsum('bclgn,bcsgn->bclsg', cm, bm)
    wts = cb[..., None] * decay * dt[:, :, None]
    y_diag = jnp.einsum('bclsgr,bcsgrp->bclgrp', wts, x)
    decay_states = jnp.exp(cs[:, :, -1:] - cs)
    xw = x * (decay_states * dt)[..., None]
    states = jnp.einsum('bcsgn,bcsgrp->bcgrpn', bm, xw)
    chunk_decay = jnp.exp(cs[:, :, -1])

    def step(carry, inp):
        st, dec = inp
        return carry * dec[..., None, None] + st, carry

    init = jnp.zeros((bsz, g_, r_, p_, n_), jnp.float32)
    _, prev = lax.scan(step, init, (jnp.moveaxis(states, 1, 0), jnp.moveaxis(chunk_decay, 1, 0)))
    prev = jnp.moveaxis(prev, 0, 1)
    y_off = jnp.einsum('bclgn,bcgrpn->bclgrp', cm, prev) * jnp.exp(cs)[..., None]
    y = y_diag + y_off + x * d_skip.astype(jnp.float32).reshape(g_, r_)[:, :, None]
    y = y.reshape(bsz, s, SSM_WIDTH).astype(z.dtype)
    yg = (y * jax.nn.silu(z)).reshape(bsz, s, g_, SSM_WIDTH // g_)
    return rmsnorm(yg, norm_g.reshape(g_, SSM_WIDTH // g_)).reshape(bsz, s, SSM_WIDTH)

def memory_cross_attention(h, mem_n, w_q, w_kv, w_o):
    bsz, s, d = h.shape
    m = mem_n.shape[1]
    q = (h @ w_q).reshape(bsz, s, XA_HEADS, XA_HEAD_DIM) * (XA_HEAD_DIM ** -0.5)
    k, v = jnp.split(mem_n @ w_kv, 2, axis=-1)
    k = k.reshape(bsz, m, XA_HEADS, XA_HEAD_DIM)
    v = v.reshape(bsz, m, XA_HEADS, XA_HEAD_DIM)
    scores = jnp.einsum('bshd,bmhd->bhsm', q, k).astype(jnp.float32)
    p = jax.nn.softmax(scores, axis=-1).astype(v.dtype)
    o = jnp.einsum('bhsm,bmhd->bshd', p, v).reshape(bsz, s, d)
    return o @ w_o

def hierarchical_moe(h, w_rg, b_rg, w_re, b_re, w_gu, w_dn):
    bsz, s, d = h.shape
    t = bsz * s
    xt = h.reshape(t, d)
    g_logits = (xt @ w_rg).astype(jnp.float32) + b_rg.astype(jnp.float32)
    grp = jnp.argmax(g_logits, axis=-1)
    p_grp = jnp.max(jax.nn.softmax(g_logits, axis=-1), axis=-1, keepdims=True)
    e_logits = ((xt @ w_re).astype(jnp.float32) + b_re.astype(jnp.float32)).reshape(t, N_EXPERT_GROUPS, EXPERTS_PER_GROUP)
    e_in = e_logits[jnp.arange(t), grp]
    top_v, top_i = lax.top_k(e_in, TOP_K_IN_GROUP)
    gate = p_grp * jax.nn.softmax(top_v, axis=-1)
    expert = grp[:, None] * EXPERTS_PER_GROUP + top_i
    n_assign = t * TOP_K_IN_GROUP
    flat_e = expert.reshape(n_assign)
    flat_tok = jnp.repeat(jnp.arange(t, dtype=jnp.int32), TOP_K_IN_GROUP)
    flat_w = gate.reshape(n_assign)
    order = jnp.argsort(flat_e)
    se, stok, sw = flat_e[order], flat_tok[order], flat_w[order]
    counts = jnp.bincount(flat_e, length=N_EXPERTS)
    starts = jnp.cumsum(counts) - counts
    padded = (counts + MOE_BLOCK - 1) // MOE_BLOCK * MOE_BLOCK
    pad_ends = jnp.cumsum(padded)
    pad_starts = pad_ends - padded
    dest = pad_starts[se] + (jnp.arange(n_assign) - starts[se])
    n_blocks = (n_assign + MOE_BLOCK - 1) // MOE_BLOCK + N_EXPERTS
    buf_len = n_blocks * MOE_BLOCK
    buf_tok = jnp.full((buf_len,), t, jnp.int32).at[dest].set(stok)
    buf_w = jnp.zeros((buf_len,), jnp.float32).at[dest].set(sw)
    block_e = jnp.minimum(jnp.searchsorted(pad_ends, jnp.arange(n_blocks) * MOE_BLOCK, side='right'), N_EXPERTS - 1)
    x_pad = jnp.concatenate([xt, jnp.zeros((1, d), xt.dtype)], axis=0)
    xb = x_pad[buf_tok].reshape(n_blocks, MOE_BLOCK, d)

    def expert_block(args):
        xblk, e = args
        gg, uu = jnp.split(xblk @ w_gu[e], 2, axis=-1)
        return (jax.nn.silu(gg) * uu) @ w_dn[e]

    yb = lax.map(expert_block, (xb, block_e)).reshape(buf_len, d)
    yb = yb * buf_w[:, None].astype(yb.dtype)
    out = jnp.zeros((t + 1, d), yb.dtype).at[buf_tok].add(yb)[:t]
    return out.reshape(bsz, s, d)

def setup_inputs(seed: int = 0) -> dict:
    key = jax.random.key(seed)
    ks = iter(jax.random.split(key, 48))

    def nrm(shape, scale):
        return jax.random.normal(next(ks), shape, jnp.float32) * scale

    def gain(shape):
        return 1.0 + nrm(shape, 0.05)

    L, D = DEPTH, D_MODEL
    inp = {}
    inp['x'] = nrm((BATCH, SEQ, D), 1.0)
    inp['mem'] = nrm((BATCH, MEM_LEN, D), 1.0)
    inp['norm_mix'] = gain((L, D))
    inp['w_in'] = nrm((L, D, IN_DIM), D ** -0.5)
    inp['conv_a_w'] = nrm((L, CONV_WIDTH, LRU_WIDTH), CONV_WIDTH ** -0.5)
    inp['conv_a_b'] = nrm((L, LRU_WIDTH), 0.02)
    inp['lru_gx_w'] = nrm((L, LRU_HEADS, LRU_HEAD_DIM, LRU_HEAD_DIM), LRU_HEAD_DIM ** -0.5)
    inp['lru_gx_b'] = nrm((L, LRU_HEADS, LRU_HEAD_DIM), 0.02)
    inp['lru_ga_w'] = nrm((L, LRU_HEADS, LRU_HEAD_DIM, LRU_HEAD_DIM), LRU_HEAD_DIM ** -0.5)
    inp['lru_ga_b'] = nrm((L, LRU_HEADS, LRU_HEAD_DIM), 0.02)
    a_c = jax.random.uniform(next(ks), (L, LRU_WIDTH), jnp.float32, 0.9, 0.999)
    p = a_c ** (1.0 / LRU_C)
    inp['lru_lambda'] = jnp.log(p) - jnp.log1p(-p)
    inp['sgu_norm'] = gain((L, SGU_WIDTH))
    inp['sgu_w'] = nrm((L, SGU_GROUPS, SGU_BLOCK, SGU_BLOCK), SGU_BLOCK ** -0.5)
    inp['sgu_b'] = gain((L, SGU_GROUPS, SGU_BLOCK))
    inp['conv_c_w'] = nrm((L, CONV_WIDTH, SSM_CONV_DIM), CONV_WIDTH ** -0.5)
    inp['conv_c_b'] = nrm((L, SSM_CONV_DIM), 0.02)
    dt0 = jnp.exp(jax.random.uniform(next(ks), (L, SSM_HEADS), jnp.float32, math.log(1e-3), math.log(1e-1)))
    inp['ssm_dt_bias'] = dt0 + jnp.log(-jnp.expm1(-dt0))
    inp['ssm_a_log'] = jnp.log(jax.random.uniform(next(ks), (L, SSM_HEADS), jnp.float32, 1.0, 16.0))
    inp['ssm_d'] = gain((L, SSM_HEADS))
    inp['ssm_norm'] = gain((L, SSM_WIDTH))
    inp['w_a_proj'] = nrm((L, LRU_WIDTH, D), LRU_WIDTH ** -0.5)
    inp['w_b_proj'] = nrm((L, SGU_WIDTH, D), SGU_WIDTH ** -0.5)
    inp['w_c_proj'] = nrm((L, SSM_WIDTH, D), SSM_WIDTH ** -0.5)
    inp['w_out'] = nrm((L, D, D), D ** -0.5)
    inp['norm_xa'] = gain((L, D))
    inp['norm_mem'] = gain((L, D))
    inp['w_q'] = nrm((L, D, D), D ** -0.5)
    inp['w_kv'] = nrm((L, D, 2 * D), D ** -0.5)
    inp['w_o'] = nrm((L, D, D), D ** -0.5)
    inp['norm_ffn'] = gain((L, D))
    inp['w_router_group'] = nrm((L, D, N_EXPERT_GROUPS), D ** -0.5)
    inp['b_router_group'] = nrm((L, N_EXPERT_GROUPS), 0.01)
    inp['w_router_expert'] = nrm((L, D, N_EXPERTS), D ** -0.5)
    inp['b_router_expert'] = nrm((L, N_EXPERTS), 0.01)
    inp['w_gate_up'] = nrm((L, N_EXPERTS, D, 2 * D_EXPERT), D ** -0.5)
    inp['w_down'] = nrm((L, N_EXPERTS, D_EXPERT, D), D_EXPERT ** -0.5)
    inp['norm_final'] = gain((D,))
    return inp

def reference(x, mem, norm_mix, w_in, conv_a_w, conv_a_b, lru_gx_w, lru_gx_b, lru_ga_w, lru_ga_b,
              lru_lambda, sgu_norm, sgu_w, sgu_b, conv_c_w, conv_c_b, ssm_dt_bias, ssm_a_log, ssm_d,
              ssm_norm, w_a_proj, w_b_proj, w_c_proj, w_out, norm_xa, norm_mem, w_q, w_kv, w_o,
              norm_ffn, w_router_group, b_router_group, w_router_expert, b_router_expert,
              w_gate_up, w_down, norm_final):
    bsz, s, d = x.shape
    for l in range(DEPTH):
        h = rmsnorm(x, norm_mix[l])
        proj = h @ w_in[l]
        xa, ya, uv, zc, xbc, dtc, gates = jnp.split(
            proj, [OFF_YA, OFF_UV, OFF_Z, OFF_XBC, OFF_DT, OFF_GATE], axis=-1)
        y_a = rglru_branch(xa, ya, conv_a_w[l], conv_a_b[l], lru_gx_w[l], lru_gx_b[l],
                           lru_ga_w[l], lru_ga_b[l], lru_lambda[l]) @ w_a_proj[l]
        y_b = sgu_branch(uv, sgu_norm[l], sgu_w[l], sgu_b[l]) @ w_b_proj[l]
        y_c = ssd_branch(zc, xbc, dtc, conv_c_w[l], conv_c_b[l], ssm_dt_bias[l], ssm_a_log[l],
                         ssm_d[l], ssm_norm[l]) @ w_c_proj[l]
        g = jax.nn.sigmoid(gates).reshape(bsz, s, N_BRANCHES, d)
        merged = g[:, :, 0] * y_a + g[:, :, 1] * y_b + g[:, :, 2] * y_c
        x = x + merged @ w_out[l]
        x = x + memory_cross_attention(rmsnorm(x, norm_xa[l]), rmsnorm(mem, norm_mem[l]),
                                       w_q[l], w_kv[l], w_o[l])
        x = x + hierarchical_moe(rmsnorm(x, norm_ffn[l]), w_router_group[l], b_router_group[l],
                                 w_router_expert[l], b_router_expert[l], w_gate_up[l], w_down[l])
    return rmsnorm(x, norm_final)


_drawn_inputs = setup_inputs


def setup_inputs(seed=0):
    import zlib

    import numpy as np

    out = dict(_drawn_inputs(seed))
    spreads = {}
    factors = {'lru_gx_b': 5.49,
     'lru_ga_b': 20.844,
     'sgu_norm': 2.794,
     'norm_xa': 4.275,
     'norm_mem': 4.224,
     'b_router_group': 30.165,
     'b_router_expert': 24.687,
     'norm_ffn': 4.354}
    for name, (base, spread) in spreads.items():
        noise = np.random.default_rng([zlib.crc32(name.encode()), seed]).standard_normal(out[name].shape)
        drawn = base * np.exp(spread * noise) if base else spread * noise
        out[name] = jnp.asarray(drawn.astype(out[name].dtype))
    for name, factor in factors.items():
        out[name] = (out[name] * factor).astype(out[name].dtype)
    return out
```

```python
import concourse.bass as bass
from concourse import mybir
from contextlib import ExitStack

P = 128


def encoder_kernel(nc, x, mem, norm_mix, w_in, conv_a_w, conv_a_b, lru_gx_w, lru_gx_b, lru_ga_w,
                   lru_ga_b, lru_lambda, sgu_norm, sgu_w, sgu_b, conv_c_w, conv_c_b, ssm_dt_bias,
                   ssm_a_log, ssm_d, ssm_norm, w_a_proj, w_b_proj, w_c_proj, w_out, norm_xa,
                   norm_mem, w_q, w_kv, w_o, norm_ffn, w_router_group, b_router_group,
                   w_router_expert, b_router_expert, w_gate_up, w_down, norm_final, out):
    F32, I32 = mybir.dt.float32, mybir.dt.int32
    ALU, ACT, AX = mybir.AluOpType, mybir.ActivationFunctionType, mybir.AxisListType

    T = x.shape[1]
    D = x.shape[2]
    KD = D // P
    NT = T // P
    EPS = 1e-6
    CONV = conv_a_w.shape[1]
    HEADS = ssm_d.shape[1]
    GROUPS = 4
    HPG = HEADS // GROUPS
    HD = D // HEADS
    XBC_TILES = conv_c_w.shape[2] // P
    OFF_YA, OFF_UV = D, 2 * D
    OFF_Z = OFF_UV + 2 * D
    OFF_XBC = OFF_Z + D
    OFF_DT = OFF_XBC + XBC_TILES * P
    OFF_GATE = OFF_DT + HEADS
    SGU_BLOCK = sgu_w.shape[2]
    SGU_G = sgu_w.shape[1]
    CHUNK = 64
    LRU_C = 8.0
    XA_HEADS = 4
    XA_DH = D // XA_HEADS
    NG, NE = w_router_group.shape[2], w_router_expert.shape[2]
    EPG = NE // NG
    DE = w_down.shape[2]
    WIN = 64
    SLOTS = 2 * T
    SLOTP = SLOTS + WIN
    NOV = SLOTS // WIN - 1
    BIG = 1e30

    order = ["ha0", "hb0", "ha1", "hb1", "par0", "par1"]
    order += ["xbc0", "xbc1", "dt0"] + [f"xbc{i}" for i in range(2, 8)] + [f"xa{i}" for i in range(4)]
    order += ["cs0"] + [f"xt{i}" for i in range(4)]
    order += ["z0", "z1"] + [f"xs{i}" for i in range(4)] + ["z2", "z3"] + [f"cb{i}" for i in range(GROUPS)]
    for i in range(4):
        order += [f"v{i}", f"lg{2 * i}", f"lg{2 * i + 1}"]
    order += ["wst0", "u0", "r0", "r1", "u1", "y0", "r2", "u2", "y1", "r3", "u3", "y2", "r4",
              "ya0", "y3", "r5", "ya1", "y4", "r6", "ya2", "y5", "r7", "ya3", "y6"]
    order += [f"sg{i}" for i in range(4)] + ["y7"]
    for b in "ABC":
        for h in (0, 2):
            order += [f"g{b}{h}", f"g{b}{h + 1}", f"p{b}{h}", f"p{b}{h + 1}"]
        if b == "A":
            order += ["cn0", "cn1"]
        if b == "B":
            order += [f"mt{i}" for i in range(4)]
    order += [f"wo{i}" for i in range(4)] + ["k0", "k1", "xn0", "k2", "k3"]
    order += [f"q{i}" for i in range(4)] + [f"sc{i}" for i in range(4)] + [f"va{i}" for i in range(4)]
    order += ["pt0", "pt1", "o0", "pt2", "o1", "pt3", "o2", "o3"]
    order += [f"ao{i}" for i in range(4)] + ["rt0"] + [f"tr{i}" for i in range(4)] + ["rk0"]
    order += [f"ga{i}" for i in range(KD)] + ["st0", "st1"]
    U = {name: i for i, name in enumerate(order)}
    NB = 8

    def family(name):
        return name.rstrip("0123456789")

    def member(name):
        return int(name[len(family(name)):])

    SLABS = [(w_in, OFF_XBC + 512 * i, f"xbc{2 * i + 1}") for i in range(4)]
    SLABS += [(w_in, 512 * i, f"xa{2 * i + 1}") for i in range(2)]
    SLABS += [(w_in, OFF_Z + 512 * i, f"z{2 * i + 1}") for i in range(2)]
    SLABS += [(w_in, OFF_UV + D + 512 * i, f"v{2 * i + 1}") for i in range(2)]
    SLABS += [(w_in, OFF_UV + 512 * i, f"u{2 * i + 1}") for i in range(2)]
    SLABS += [(w_in, OFF_YA + 512 * i, f"ya{2 * i + 1}") for i in range(2)]
    for b, w in enumerate((w_a_proj, w_b_proj, w_c_proj)):
        for h in range(2):
            SLABS += [(w_in, OFF_GATE + b * D + 512 * h, f"g{'ABC'[b]}{2 * h + 1}"),
                      (w, 512 * h, f"p{'ABC'[b]}{2 * h + 1}")]
    for w, c0, name in ((w_out, 0, "wo"), (w_kv, 0, "k"), (w_q, 0, "q"), (w_kv, D, "va"), (w_o, 0, "ao")):
        SLABS += [(w, c0 + 512 * h, f"{name}{2 * h + 1}") for h in range(2)]
    NSLAB = len(SLABS)
    SLAB_OF = {last: n for n, (_, _, last) in enumerate(SLABS)}
    PRE = 3
    RING = 6
    PREFILLS = NSLAB // PRE
    assert NSLAB % PRE == 0

    ctx = ExitStack()
    with ctx:
        def sb(name, shape, dt=F32):
            return ctx.enter_context(nc.sbuf_tensor(name, shape, dt))

        ring = sb("ring", [P, RING, KD * 512])
        blk = sb("blk", [P, 9, KD * T])

        def block(i):
            if i < 9:
                return blk[:, i, :]
            return ring[:, PRE + (i - 9) // 2, (i - 9) % 2 * 2048:(i - 9) % 2 * 2048 + 2048]

        def asT(i):
            return block(i).rearrange("p (f t) -> p f t", t=T)

        def asN(i):
            return block(i).rearrange("p (t f) -> p t f", t=NT)

        hT, hxT = asT(0), asT(0)
        xT = asT(1)
        xN, vN, memT, x2N = asN(2), asN(2), asT(2), asN(2)
        xnN, xaT, memnN = asN(3), asT(3), asN(3)
        uT, KT = asT(4), asT(4)
        yaT, memN, VN = asT(5), asN(5), asN(5)
        junk, a2T, mergedT, oT, outN = asN(6), asT(6), asT(6), asT(6), asN(6)
        gateT, QT = asT(7), asT(7)
        ycT, x1sq, x2sq = asT(8), asT(8), asT(8)
        h3N = asN(6)
        xsN, zT, gxT, aT, csq = asN(11), asT(12), asT(13), asT(14), asT(13)

        def xbcT(f):
            return asT(9 + f // KD)[:, f % KD, :]

        probs = block(3).rearrange("p (h t m) -> p h t m", h=XA_HEADS, t=NT)
        probsT = block(8).rearrange("p (h j t) -> p h j t", h=XA_HEADS, j=NT)
        sel = block(0)[:, 0:NT * SLOTS].rearrange("p (t s) -> p t s", t=NT)
        selw = block(0)[:, NT * SLOTS:2 * NT * SLOTS].rearrange("p (t s) -> p t s", t=NT)
        seltmp = block(7)[:, 0:SLOTS]
        slotsT = blk[:, 3:6, :].rearrange("p b n -> p (b n)")[:, 0:KD * SLOTP].rearrange("p (k s) -> p k s", k=KD)
        yT = blk[:, 6:9, :].rearrange("p b n -> p (b n)")[:, 0:KD * SLOTP].rearrange("p (k s) -> p k s", k=KD)
        ySN = blk[:, 3:5, :].rearrange("p b n -> p (b n)").rearrange("p (s d) -> p s d", d=D)
        junk3 = asN(5)
        scat = blk[:, 1, 0:1024].rearrange("p (s t) -> p s t", t=T)
        xe = blk[:, 1, 1024:2048].rearrange("p (b k w) -> p b k w", b=2, w=WIN)

        ident = sb("ident", [P, P])
        ones = sb("ones", [P, P])
        onesm = sb("onesm", [P, P])
        mask = sb("mask", [P, 3 * P])
        strict = sb("strict", [P, P])
        iota_i = sb("iota_i", [P, SLOTS], I32)
        iota_f = sb("iota_f", [P, SLOTS])
        epsc = sb("epsc", [P, 1])
        prow = sb("prow", [P, 2, P])
        par = sb("par", [P, 2, P])
        wdt = sb("wdt", [P, KD, HEADS])
        wr = sb("wr", [P, KD, NG + NE])
        br = sb("br", [P, NG + NE])
        gxw = sb("gxw", [P, KD, P])
        gaw = sb("gaw", [P, KD, P])
        sguw = sb("sguw", [P, SGU_G, P])
        sguwT = sb("sguwT", [P, SGU_G, P])
        sgub = sb("sgub", [P, SGU_G, P])
        dtb = sb("dtb", [P, HEADS])
        alog = sb("alog", [P, HEADS])
        dsk = sb("dsk", [P, HEADS])
        dcol = sb("dcol", [P, KD])
        stat = sb("stat", [P, 32])
        c8 = sb("c8", [P, 6, KD])
        dtw = sb("dtw", [P, 7, NT * HEADS])
        csN = sb("csN", [P, NT, HEADS])
        cbm = sb("cbm", [P, GROUPS, 3 * P])
        dec = sb("dec", [P, 2, 2, 3 * P])
        bnst = sb("bnst", [P, NT, 2, 6])
        bnag = sb("bnag", [P, NT, 2])
        sq3 = sb("sq3", [P, 2 * NT])
        sm = sb("sm", [P, 4, XA_HEADS * NT])
        decflat = dec[:, :, :, :].rearrange("p a b c -> p (a b c)")
        crms = decflat[:, 0:GROUPS * T].rearrange("p (g t) -> p g t", t=T)
        x1rms = decflat[:, GROUPS * T:(GROUPS + 1) * T]
        gfin = decflat[:, 0:D]
        cflat = cbm[:, :, :].rearrange("p g c -> p (g c)")
        NF = DE // P
        SEG = DE // 2
        sil = cflat[:, 0:2 * SEG].rearrange("p (b f) -> p b f", b=2)
        hm = cflat[:, 2 * SEG:4 * SEG].rearrange("p (b f) -> p b f", b=2)
        hmT = cflat[:, 4 * SEG:6 * SEG].rearrange("p (b j c) -> p b j c", b=2, c=P)
        yS = decflat[:, D:D + 512]
        NCAND = (T // WIN - 1) * NE
        ovf = blk[0:1, 7:9, :].rearrange("p b n -> p (b n)")[:, 1536:1536 + (10 + 2 * NOV) * NCAND]
        starts_i = sb("starts_i", [1, NE + 1], I32)
        ov_i = sb("ov_i", [1, 2 * NOV + 2], I32)

        psum = [ctx.enter_context(nc.psum_tensor(f"bank{i}", [P, 512], F32)) for i in range(NB)]

        def bank(name):
            return psum[U[name] % NB]

        def sems(names):
            return {n: ctx.enter_context(nc.semaphore(n)) for n in names.split()}

        sem = sems("""eps x_loaded par_loaded small_loaded mem_loaded gfin_loaded out_stored fills consts
            act_step dve_step unit_done x_rms xn_ready
            conv_init silu_ready lam_ln alog_exp dt_ready dt_act dta_ready d_ready c_ready
            ln_var ln_rms vn_ready a2_ready a_ready a2_min mult_ready yA_ready
            exp_ready w_ready yz_ready csq_ready  yC_ready merged_B merged_C
            mem_rms memn_ready x1sq_ready hx_ready smax_ready p_ready
            wr_ready x2sq_ready x2_rms x2_rinv h3_ready gexp_in gexp_done texp_in texp_done assign_ready sel_ready selw_ready
             ov_ready pad_ready half_done gu_done turn_done dn_done yturn_done xe_ready
            esilu_ready h_ready hT_ready yS_ready y_slots ySNa_ready ySNb_ready y_complete x3sq_ready x3sum_ready ysn_ready fin_done x3_ready x3_rms o_final""")
        read = {f: ctx.enter_context(nc.semaphore(f + "_read"))
                for f in sorted({family(n) for n in order})}
        filled = [ctx.enter_context(nc.semaphore(f"slot_filled{i}")) for i in range(RING)]

        def tiles(vector):
            return vector.rearrange("(f p) -> f p", p=P)

        rows, pcol, npar = [], {}, 0
        for name, ap, n in (("ccw", conv_c_w[0].rearrange("k (f p) -> (k f) p", p=P), CONV * XBC_TILES),
                            ("ccb", tiles(conv_c_b[0]), XBC_TILES),
                            ("caw", conv_a_w[0].rearrange("k (f p) -> (k f) p", p=P), CONV * KD),
                            ("cab", tiles(conv_a_b[0]), KD), ("gmix", tiles(norm_mix[0]), KD),
                            ("gxb", lru_gx_b[0], KD), ("gab", lru_ga_b[0], KD),
                            ("lam", tiles(lru_lambda[0]), KD), ("gsgu", tiles(sgu_norm[0]), KD),
                            ("gssm", tiles(ssm_norm[0]), KD), ("gxa", tiles(norm_xa[0]), KD),
                            ("gmem", tiles(norm_mem[0]), KD), ("gffn", tiles(norm_ffn[0]), KD)):
            assert npar // P == (npar + n - 1) // P
            rows.append((npar // P, npar % P, ap, n))
            pcol[name] = npar
            npar += n

        def col(name, i=0):
            c = pcol[name] + i
            return par[:, c // P, c % P:c % P + 1]

        def cols(name, n):
            c = pcol[name]
            return par[:, c // P, c % P:c % P + n]

        def spread(ap):
            return ap.partition_broadcast(P)

        small = [(wdt[:], w_in[0].rearrange("(k p) n -> p k n", p=P)[:, :, OFF_DT:OFF_DT + HEADS]),
                 (dtb[:], spread(ssm_dt_bias[0])), (alog[:], spread(ssm_a_log[0])), (dsk[:], spread(ssm_d[0])),
                 (gxw[:], lru_gx_w[0].rearrange("h i j -> i h j")), (gaw[:], lru_ga_w[0].rearrange("h i j -> i h j")),
                 (sguw[:], sgu_w[0].rearrange("g t s -> t g s")), (sgub[:], spread(sgu_b[0])),
                 (wr[:, :, 0:NG], w_router_group[0].rearrange("(k p) n -> p k n", p=P)),
                 (wr[:, :, NG:], w_router_expert[0].rearrange("(k p) n -> p k n", p=P)),
                 (br[:, 0:NG], spread(b_router_group[0])), (br[:, NG:], spread(b_router_expert[0]))]

        rtl, used = {}, 0
        for name, n in (("l", NT * (NG + NE)), ("lg", NT * NG), ("le", NT * NE), ("rev", NE), ("mx", NT),
                        ("eq", NT * NE), ("key", NT * NE), ("km", NT), ("gm", NT * NG), ("gneg", NT * NG),
                        ("em", NT * NE), ("m1", NT), ("m2", NT), ("o1", NT * NE), ("o2", NT * NE), ("gs", NT),
                        ("dl", NT * NG), ("ge", NT * NG), ("dm", NT), ("te", NT), ("w1", NT), ("w2", NT),
                        ("as", NT * NE), ("cnt", NE), ("incl", NE), ("st", NE), ("pos", NT * NE),
                        ("pp", NT * NE), ("p1", NT), ("p2", NT), ("mxg", NT)):
            rtl[name] = (used, n)
            used += n
        assert SLOTS + used <= 1536
        rt = block(7)[:, SLOTS:SLOTS + used]

        def rv(name):
            a, n = rtl[name]
            return rt[:, a:a + n]

        def rt2(name):
            return rv(name).rearrange("p (t n) -> p t n", t=NT)

        block_ = ctx.enter_context(nc.Block())

        @block_.sync
        def _(sp):
            def slab(n):
                w, c0, _ = SLABS[n]
                if n >= PRE:
                    sp.wait_ge(sem["unit_done"], U[SLABS[n - PRE][2]] + 1)
                sp.dma_start(ring[:, n % PRE, :].rearrange("p (k n) -> p k n", k=KD),
                             w[0].rearrange("(k p) n -> p k n", p=P)[:, :, c0:c0 + 512]
                             ).then_inc(filled[n % PRE], 16)

            def part(e, j, s0):
                if j < 2:
                    src = w_gate_up[0, bass.ds(e, 1)].rearrange("a (k p) n -> p (a k) n", p=P)[:, 4 * j:4 * j + 4, :]
                else:
                    src = w_down[0, bass.ds(e, 1)].rearrange("a (k p) n -> p (a k) n", p=P)
                sp.dma_start(ring[:, s0 + j, :].rearrange("p (k n) -> p k n", k=4), src).then_inc(filled[s0 + j], 16)

            for t in range(NT):
                sp.dma_start(xN[:, t, :], x[0, t * P:(t + 1) * P, :]).then_inc(sem["x_loaded"], 16)
            for tile, row, ap, n in rows:
                sp.dma_start(prow[row:row + n, tile, :], ap).then_inc(sem["par_loaded"], 16)
            early = SLAB_OF["wo1"]
            for n in range(early):
                slab(n)
            sp.wait_ge(sem["unit_done"], U["pC0"] + 1)
            for j in range(3):
                part(1, j, PRE)
            for n in range(early, NSLAB):
                slab(n)
            for j in range(3):
                sp.wait_ge(sem["unit_done"], U[SLABS[NSLAB - PRE + j][2]] + 1)
                part(0, j, 0)
            with sp.Fori(1, NE // 2) as i:
                for p in range(2):
                    for j, use in enumerate(("half_done", "gu_done", "dn_done")):
                        sp.wait_ge(sem[use], i * 2 + (p - 1))
                        part(i * 2 + p, j, PRE * p)
            sp.wait_ge(sem["ov_ready"], 1)
            n_ov = sp.value_load(ov_i[0:1, 0:1], min_val=0, max_val=NOV)
            with sp.If(n_ov > 0):
                with sp.Fori(0, n_ov) as o:
                    e = sp.value_load(ov_i[0:1, bass.ds(o + 1, 1)], min_val=0, max_val=NE - 1)
                    for j, use in enumerate(("half_done", "gu_done", "dn_done")):
                        sp.wait_ge(sem[use], o + NE)
                        part(e, j, 0)
            for i in range(2 * NT):
                t, c = i // 2, slice(i % 2 * 512, (i % 2 + 1) * 512)
                sp.wait_ge(sem["o_final"], i + 1)
                sp.dma_start(out[0, t * P:(t + 1) * P, c], outN[:, t, c]).then_inc(sem["out_stored"], 16)
            sp.wait_ge(sem["out_stored"], 16 * 2 * NT)

        @block_.gpsimd
        def _(pool):
            g = nc.gpsimd
            g.memset(epsc[:], EPS).then_inc(sem["eps"], 1)
            g.memset(ident[:], 0.0)
            g.memset(ones[:], 1.0)
            g.memset(onesm[:], 1.0 / D)
            g.memset(mask[:], 1.0)
            g.memset(strict[:], 1.0)
            g.memset(sguwT[:], 0.0)
            g.iota(iota_i[:], pattern=[[1, SLOTS]], base=0, channel_multiplier=0).then_inc(sem["fills"], 1)
            pool.wait_ge(sem["fills"], 1)
            g.affine_select(out=ident[:], in_=ident[:], compare_op=ALU.not_equal, fill=1.0, base=0,
                            pattern=[[-1, P]], channel_multiplier=1)
            for c in (0, 2):
                g.affine_select(out=mask[:, c * P:(c + 1) * P], in_=mask[:, c * P:(c + 1) * P],
                                compare_op=ALU.is_ge, fill=0.0, base=0, pattern=[[1, P]], channel_multiplier=-1)
            g.affine_select(out=strict[:], in_=strict[:], compare_op=ALU.is_ge, fill=0.0, base=-1,
                            pattern=[[1, P]], channel_multiplier=-1)
            g.tensor_copy(iota_f[:], iota_i[:]).then_inc(sem["consts"], 1)
            pool.wait_ge(read["y"], KD)
            pool.wait_ge(read["z"], 4)
            g.tensor_tensor(out=ycT, in0=ycT, in1=zT, op=ALU.mult).then_inc(sem["yz_ready"], 1)
            pool.wait_ge(sem["unit_done"], U["o3"] + 1)
            g.memset(slotsT[:, :, SLOTS:SLOTP], 0.0).then_inc(sem["pad_ready"], 1)

        @block_.scalar
        def _(act):
            a = nc.scalar
            step = [0]

            def link(ins):
                step[0] += 1
                ins.then_inc(sem["act_step"], 1)
                act.wait_ge(sem["act_step"], step[0])

            def take(name):
                act.wait_ge(sem["unit_done"], U[name] + 1)
                return bank(name)

            def halves(ps):
                return ps[:, :].rearrange("p (f t) -> p f t", f=2)

            def warm(func, c):
                a.activation(stat[:, c:c + 1], epsc[:], func)

            act.wait_ge(sem["eps"], 1)
            warm(ACT.Sqrt, 28)
            act.wait_ge(sem["x_loaded"], 16 * NT)
            for t in range(NT):
                last = a.activation(junk[:, t, :], xN[:, t, :], ACT.Square, accum_out=stat[:, t:t + 1])
            link(last)
            a.activation(stat[:, 2:4], stat[:, 0:2], ACT.Sqrt, bias=epsc[:], scale=1.0 / D).then_inc(sem["x_rms"], 1)
            for dst, ap in small:
                act.dma_start(dst, ap).then_inc(sem["small_loaded"], 16)
            for i in range(2):
                ps = take(f"par{i}")
                n = min(P, npar - i * P)
                a.copy(par[:, i, 0:n], ps[:, 0:n]).then_inc(read["par"], 1)
            act.wait_ge(read["par"], 2)
            for i in range(2):
                ps = take(f"ha{i}")
                for f in range(2):
                    last = a.activation(hT[:, 4 * i + f, :], ps[:, f * T:(f + 1) * T], ACT.Copy,
                                        scale=col("gmix", 4 * i + f))
                last.then_inc(read["ha"], 1)

            def conv_init(unit, w, b, f0, acc):
                ps = take(unit)
                for f in range(2):
                    last = a.activation(acc(f0 + f), ps[:, f * T:(f + 1) * T], ACT.Identity,
                                        bias=b(f0 + f), scale=w(f0 + f))
                last.then_inc(sem["conv_init"], 1)

            def silu_xbc(i):
                act.wait_ge(read["xbc"], i + 1)
                for f in range(2 * i, 2 * i + 2):
                    last = a.activation(xbcT(f), xbcT(f), ACT.Silu)
                last.then_inc(sem["silu_ready"], 1)

            link(a.activation(c8[:, 0, :], cols("lam", KD), ACT.Abs))
            link(a.activation(c8[:, 1, :], c8[:, 0, :], ACT.Exp, scale=-1.0))
            a.activation(c8[:, 2, :], c8[:, 1, :], ACT.Ln, bias=1.0).then_inc(sem["lam_ln"], 1)
            act.wait_ge(sem["small_loaded"], 16 * len(small))
            a.activation(dtw[:, 5, 0:HEADS], alog[:], ACT.Exp).then_inc(sem["alog_exp"], 1)
            NX = XBC_TILES // 2
            for i in range(NX):
                conv_init(f"xbc{i}", lambda f: col("ccw", 3 * XBC_TILES + f), lambda f: col("ccb", f), 2 * i, xbcT)
                if i == 2:
                    act.wait_ge(sem["dt_ready"], 1)
                    link(a.activation(dtw[:, 1, :], dtw[:, 0, :], ACT.Abs))
                    link(a.activation(dtw[:, 2, :], dtw[:, 1, :], ACT.Exp, scale=-1.0))
                    a.activation(dtw[:, 3, :], dtw[:, 2, :], ACT.Ln, bias=1.0).then_inc(sem["dt_act"], 1)
                if i >= 2:
                    silu_xbc(i - 2)
            for i in range(KD // 2):
                conv_init(f"xa{i}", lambda f: col("caw", 3 * KD + f), lambda f: col("cab", f), 2 * i,
                          lambda f: xaT[:, f, :])
                if i < 2:
                    silu_xbc(NX - 2 + i)

            def evac(name, dst, func, scale=1.0):
                ps = take(name)
                i = 2 * member(name)
                a.activation(dst[:, i:i + 2, :], halves(ps), func, scale=scale).then_inc(read[family(name)], 1)

            for i in range(2):
                evac(f"z{i}", zT, ACT.Silu)
            for i in range(4):
                ps = take(f"xs{i}")
                a.copy(xsN[:, i // 2, i % 2 * 512:(i % 2 + 1) * 512], ps[:, :]).then_inc(read["xs"], 1)
            for i in range(2, 4):
                evac(f"z{i}", zT, ACT.Silu)
            for i in range(4):
                ps = take(f"v{i}")
                a.activation(vN[:, i % 2, i // 2 * 512:(i // 2 + 1) * 512], ps[:, :],
                             ACT.Gelu_apprx_tanh).then_inc(read["v"], 1)
                for j in (2 * i, 2 * i + 1):
                    ps = take(f"lg{j}")
                    a.activation(gxT[:, j, :], ps[:, 0:T], ACT.Sigmoid, bias=col("gxb", j))
                    a.activation(aT[:, j, :], ps[:, T:2 * T], ACT.Sigmoid, bias=col("gab", j)).then_inc(read["lg"], 1)
            ps = take("wst0")
            wT = ps[:, :].rearrange("p (g t) -> p g t", g=SGU_G)
            a.copy(sguwT[0:CHUNK, :, :], wT[0:CHUNK])
            a.copy(sguwT[CHUNK:P, :, CHUNK:P], wT[CHUNK:P, :, CHUNK:P]).then_inc(read["wst"], 1)
            act.wait_ge(sem["c_ready"], 1)
            act.wait_ge(read["lg"], KD)
            for j in range(KD):
                last = a.activation(a2T[:, j, :], aT[:, j, :], ACT.Exp, scale=c8[:, 5, j:j + 1])
            last.then_inc(sem["a2_ready"], 1)
            act.wait_ge(sem["a2_ready"], 1)
            for j in range(KD):
                last = a.activation(aT[:, j, :], aT[:, j, :], ACT.Exp, scale=c8[:, 4, j:j + 1])
            last.then_inc(sem["a_ready"], 1)

            def exps(i):
                act.wait_ge(read["r"], i + 1)
                v = dec[:, i % 2].rearrange("p h c -> p (h c)")
                a.activation(v, v, ACT.Exp).then_inc(sem["exp_ready"], 1)

            exps(0)
            exps(1)
            evac("u0", uT, ACT.Gelu_apprx_tanh)
            act.wait_ge(sem["a2_min"], 1)
            a.activation(a2T, a2T, ACT.Sqrt, bias=1.0, scale=-1.0).then_inc(sem["mult_ready"], 1)
            act.wait_ge(sem["ln_var"], 1)
            a.activation(stat[:, 8:10], bnag[:, :, 1], ACT.Sqrt, bias=epsc[:]).then_inc(sem["ln_rms"], 1)
            for i in range(1, 4):
                evac(f"u{i}", uT, ACT.Gelu_apprx_tanh)
                exps(i + 1)
            for i in range(4):
                evac(f"ya{i}", yaT, ACT.Gelu_apprx_tanh)
                if i < 3:
                    exps(5 + i)

            def gates(b, h):
                for i in (2 * h, 2 * h + 1):
                    if b == 1:
                        act.wait_ge(read["pA"], i + 1)
                    if b == 2:
                        act.wait_ge(sem["merged_B"], i + 1)
                    evac(f"g{'ABC'[b]}{i}", gateT, ACT.Sigmoid)

            gates(0, 0)
            act.wait_ge(sem["yz_ready"], 1)
            act.wait_ge(sem["yA_ready"], 1)
            a.activation(csq, ycT, ACT.Square).then_inc(sem["csq_ready"], 1)
            gates(0, 1)
            for i in range(2):
                ps = take(f"cn{i}")
                a.activation(crms[:, 2 * i:2 * i + 2, :], halves(ps), ACT.Sqrt, bias=epsc[:],
                             scale=float(GROUPS)).then_inc(read["cn"], 1)
            act.wait_ge(sem["unit_done"], U["pA3"] + 1)
            act.dma_start(memN, mem[0].rearrange("(t p) f -> p t f", p=P)).then_inc(sem["mem_loaded"], 16)
            gates(1, 0)
            act.wait_ge(sem["mem_loaded"], 16)
            for t in range(NT):
                last = a.activation(memnN[:, t, :], memN[:, t, :], ACT.Square, accum_out=stat[:, 10 + t:11 + t])
            link(last)
            a.activation(stat[:, 12:14], stat[:, 10:12], ACT.Sqrt, bias=epsc[:], scale=1.0 / D
                         ).then_inc(sem["mem_rms"], 1)
            gates(1, 1)
            gates(2, 0)
            gates(2, 1)
            act.wait_ge(sem["unit_done"], U["pC3"] + 1)
            for i in range(4):
                act.wait_ge(read["wo"], i + 1)
                a.activation(x1sq[:, 2 * i:2 * i + 2, :], xT[:, 2 * i:2 * i + 2, :], ACT.Square
                             ).then_inc(sem["x1sq_ready"], 1)
            for i in range(2):
                evac(f"k{i}", KT, ACT.Copy)
            ps = take("xn0")
            a.activation(x1rms, ps[:, 0:T], ACT.Sqrt, bias=epsc[:]).then_inc(read["xn"], 1)
            for i in range(2, 4):
                evac(f"k{i}", KT, ACT.Copy)
            for i in range(4):
                evac(f"q{i}", QT, ACT.Copy, scale=float(XA_DH) ** -0.5)
            for h in range(XA_HEADS):
                ps = take(f"sc{h}")
                act.wait_ge(sem["smax_ready"], h + 1)
                for t in range(NT):
                    c = NT * h + t
                    last = a.activation(probs[:, h, t, :], ps[:, t * T:(t + 1) * T], ACT.Exp,
                                        bias=sm[:, 1, c:c + 1], accum_out=sm[:, 2, c:c + 1])
                last.then_inc(read["sc"], 1)
            for i in range(4):
                ps = take(f"va{i}")
                a.copy(VN[:, i % 2, i // 2 * 512:(i // 2 + 1) * 512], ps[:, :]).then_inc(read["va"], 1)
            for h in range(XA_HEADS):
                ps = take(f"pt{h}")
                a.copy(probsT[:, h, :, :], halves(ps)).then_inc(read["pt"], 1)
            warm(ACT.Sqrt, 29)
            for i in range(4):
                act.wait_ge(read["ao"], i + 1)
                a.activation(x2sq[:, 2 * i:2 * i + 2, :], xT[:, 2 * i:2 * i + 2, :], ACT.Square
                             ).then_inc(sem["x2sq_ready"], 1)
            ps = take("rt0")
            a.activation(stat[:, 18:20], ps[:, 128:128 + NT], ACT.Sqrt, bias=epsc[:], scale=1.0 / D
                         ).then_inc(sem["x2_rms"], 1)
            for i in range(4):
                ps = take(f"tr{i}")
                a.copy(x2N[:, i % 2, i // 2 * 512:(i // 2 + 1) * 512], ps[:, :]).then_inc(read["tr"], 1)
            act.wait_ge(sem["gexp_in"], 1)
            a.activation(rv("ge"), rv("dl"), ACT.Exp).then_inc(sem["gexp_done"], 1)
            act.wait_ge(sem["texp_in"], 1)
            a.activation(rv("te"), rv("dm"), ACT.Exp).then_inc(sem["texp_done"], 1)
            act.wait_ge(sem["x2_rinv"], 1)
            act.wait_ge(read["tr"], 4)
            for t in range(NT):
                last = a.activation(h3N[:, t, :], x2N[:, t, :], ACT.Copy, scale=stat[:, 20 + t:21 + t])
            last.then_inc(sem["h3_ready"], 1)
            act.dma_start(gfin, norm_final.partition_broadcast(P)).then_inc(sem["gfin_loaded"], 16)
            for k in range(KD):
                ps = take(f"ga{k}")
                a.activation(slotsT[:, k, 0:SLOTS], ps[:, :], ACT.Copy, scale=col("gffn", k)).then_inc(read["ga"], 1)
            for i in range(2):
                ps = take(f"st{i}")
                a.copy(scat[:, 2 * i:2 * i + 2, :], halves(ps)).then_inc(read["st"], 1)

            def window_act(n, p):
                act.wait_ge(sem["gu_done"], n + 1)
                a.activation(sil[:, p], psum[4 * p][:, 0:SEG], ACT.Silu).then_inc(sem["esilu_ready"], 1)
                act.wait_ge(sem["turn_done"], n + 1)
                a.copy(hmT[:, p], psum[4 * p + 1][:, 0:2 * P].rearrange("p (j c) -> p j c", c=P)
                       ).then_inc(sem["hT_ready"], 1)
                act.wait_ge(sem["dn_done"], n + 1)
                a.copy(yS, psum[4 * p + 2][:, :]).then_inc(sem["yS_ready"], 1)

            with act.Fori(0, NE // 2) as i:
                for p in range(2):
                    window_act(i * 2 + p, p)
            act.wait_ge(sem["ov_ready"], 1)
            n_ov = act.value_load(ov_i[0:1, 0:1], min_val=0, max_val=NOV)
            with act.If(n_ov > 0):
                with act.Fori(0, n_ov) as o:
                    window_act(o + NE, 0)
            warm(ACT.Sqrt, 31)
            for n in range(SLOTS // P):
                act.wait_ge(sem["ysn_ready"], 2 * n + 1)
                a.copy(ySN[:, n, 0:512], psum[2 * n][:, :]).then_inc(sem["ySNa_ready"], 1)
            for i in range(2 * NT):
                t, h = i // 2, i % 2
                c = slice(h * 512, (h + 1) * 512)
                act.wait_ge(sem["x3_ready"], i + 1)
                last = a.activation(junk3[:, t, c], x2N[:, t, c], ACT.Square, accum_out=sq3[:, i:i + 1])
                if h:
                    last.then_inc(sem["x3sq_ready"], 1)
                    act.wait_ge(sem["x3sum_ready"], t + 1)
                    a.activation(stat[:, 24 + t:25 + t], stat[:, 22 + t:23 + t], ACT.Sqrt, bias=epsc[:],
                                 scale=1.0 / D).then_inc(sem["x3_rms"], 1)

        @block_.vector
        def _(dve):
            v = nc.vector
            step = [0]

            def link(ins):
                step[0] += 1
                ins.then_inc(sem["dve_step"], 1)
                dve.wait_ge(sem["dve_step"], step[0])

            def take(name):
                dve.wait_ge(sem["unit_done"], U[name] + 1)
                return bank(name)

            def halves(ps):
                return ps[:, :].rearrange("p (f t) -> p f t", f=2)

            dve.wait_ge(sem["x_rms"], 1)
            link(v.reciprocal(stat[:, 4:6], stat[:, 2:4]))
            for t in range(NT):
                v.tensor_scalar(xnN[:, t, :], xN[:, t, :], stat[:, 4 + t:5 + t], None, ALU.mult
                                ).then_inc(sem["xn_ready"], 1)
            dve.wait_ge(read["par"], 2)
            for i in range(2):
                ps = take(f"hb{i}")
                for f in range(2):
                    last = v.tensor_scalar(hT[:, 4 * i + 2 + f, :], ps[:, f * T:(f + 1) * T],
                                           col("gmix", 4 * i + 2 + f), None, ALU.mult)
                last.then_inc(read["hb"], 1)
            link(v.tensor_scalar(c8[:, 3, :], cols("lam", KD), -1.0, 0.0, ALU.mult, ALU.max))
            dve.wait_ge(sem["lam_ln"], 1)
            link(v.tensor_tensor(c8[:, 3, :], c8[:, 3, :], c8[:, 2, :], ALU.add))
            v.tensor_scalar(c8[:, 4, :], c8[:, 3, :], -LRU_C, None, ALU.mult)
            v.tensor_scalar(c8[:, 5, :], c8[:, 3, :], -2 * LRU_C, None, ALU.mult).then_inc(sem["c_ready"], 1)
            dve.wait_ge(sem["small_loaded"], 16 * len(small))
            pairs = dsk[:, :].rearrange("p (f h) -> p f h", h=P // HD)
            for h in range(P // HD):
                last = v.tensor_copy(dcol[h * HD:(h + 1) * HD, :], pairs[h * HD:(h + 1) * HD, :, h])
            last.then_inc(sem["d_ready"], 1)
            for k in range(KD):
                last = v.tensor_scalar(wr[:, k, :], wr[:, k, :], col("gffn", k), None, ALU.mult)
            last.then_inc(sem["wr_ready"], 1)

            convs = [0]

            def taps(unit, w, tiles_, f0, acc):
                convs[0] += 1
                dve.wait_ge(sem["conv_init"], convs[0])
                ps = bank(unit)
                for j in range(1, CONV):
                    for f in range(2):
                        last = v.scalar_tensor_tensor(
                            out=acc(f0 + f)[:, j:], in0=ps[:, f * T:(f + 1) * T - j],
                            scalar=col(w, (CONV - 1 - j) * tiles_ + f0 + f), in1=acc(f0 + f)[:, j:],
                            op0=ALU.mult, op1=ALU.add)
                    if j < CONV - 1:
                        link(last)
                last.then_inc(read[family(unit)], 1)

            NX = XBC_TILES // 2
            for i in range(NX):
                taps(f"xbc{i}", "ccw", XBC_TILES, 2 * i, xbcT)
                if i == 1:
                    ps = take("dt0")
                    last = (v.tensor_tensor(dtw[:, 0, :].rearrange("p (t h) -> p t h", t=NT),
                                         ps[:, 0:NT * HEADS].rearrange("p (t h) -> p t h", t=NT),
                                         dtb[:, :].rearrange("p (o h) -> p o h", o=1).to_broadcast([P, NT, HEADS]),
                                         ALU.add))
                    last.then_inc(read["dt"], 1)
                    dve.wait_ge(read["dt"], 1)
                    v.tensor_scalar(dtw[:, 4, :], dtw[:, 0, :], 0.0, None, ALU.max).then_inc(sem["dt_ready"], 1)
                if i == 4:
                    dve.wait_ge(sem["dt_act"], 1)
                    link(v.tensor_tensor(dtw[:, 4, :], dtw[:, 4, :], dtw[:, 3, :], ALU.add))
                    dve.wait_ge(sem["alog_exp"], 1)
                    for t in range(NT):
                        c = slice(t * HEADS, (t + 1) * HEADS)
                        last = v.scalar_tensor_tensor(out=dtw[:, 6, c], in0=dtw[:, 4, c], scalar=-1.0,
                                                      in1=dtw[:, 5, 0:HEADS], op0=ALU.mult, op1=ALU.mult)
                    last.then_inc(sem["dta_ready"], 1)
            for i in range(KD // 2):
                taps(f"xa{i}", "caw", KD, 2 * i, lambda f: xaT[:, f, :])
            ps = take("cs0")
            v.tensor_copy(csN[:, :, :], ps[:, 0:NT * HEADS].rearrange("p (t h) -> p t h", t=NT)
                          ).then_inc(read["cs"], 1)
            for i in range(4):
                ps = take(f"xt{i}")
                v.tensor_copy(xT[:, 2 * i:2 * i + 2, :], halves(ps)).then_inc(read["xt"], 1)
            for g in range(GROUPS):
                ps = take(f"cb{g}")
                v.tensor_tensor(cbm[:, g, :], ps[:, 0:3 * P], mask[:, :], ALU.mult).then_inc(read["cb"], 1)

            dve.wait_ge(read["lg"], KD)
            link(v.tensor_tensor(gxT, gxT, xaT, ALU.mult))
            def exponents(i):
                ps = take(f"r{i}")
                if i >= 2:
                    dve.wait_ge(sem["unit_done"], U[f"y{i - 2}"] + 1)
                for h in range(2):
                    c = csN[:, :, 2 * i + h:2 * i + h + 1]
                    v.tensor_scalar(dec[:, i % 2, h, 0:T], ps[:, h * T:(h + 1) * T], c[:, 0, :], 0.0,
                                    ALU.subtract, ALU.min)
                    last = v.tensor_scalar(dec[:, i % 2, h, T:], ps[:, h * T + P:(h + 1) * T], c[:, 1, :], 0.0,
                                           ALU.subtract, ALU.min)
                last.then_inc(read["r"], 1)

            def weights(i):
                dve.wait_ge(sem["exp_ready"], i + 1)
                for h in range(2):
                    hd = 2 * i + h
                    for t, c in ((0, slice(0, T)), (1, slice(T, 3 * P))):
                        last = v.scalar_tensor_tensor(
                            out=dec[:, i % 2, h, c], in0=dec[:, i % 2, h, c],
                            scalar=dtw[:, 4, t * HEADS + hd:t * HEADS + hd + 1], in1=cbm[:, hd // HPG, c],
                            op0=ALU.mult, op1=ALU.mult)
                last.then_inc(sem["w_ready"], 1)

            def skip(i):
                ps = take(f"y{i}")
                v.scalar_tensor_tensor(out=ycT[:, i, :], in0=xbcT(i), scalar=dcol[:, i:i + 1], in1=ps[:, 0:T],
                                       op0=ALU.mult, op1=ALU.add).then_inc(read["y"], 1)

            dve.wait_ge(read["cs"], 1)
            dve.wait_ge(read["cb"], GROUPS)
            exponents(0)
            exponents(1)
            weights(0)
            skip(0)
            exponents(2)
            dve.wait_ge(sem["a2_ready"], 1)
            v.tensor_scalar(a2T, a2T, 1.0, None, ALU.min).then_inc(sem["a2_min"], 1)
            dve.wait_ge(read["v"], 4)
            for t in range(NT):
                for h in range(2):
                    last = v.bn_stats(bnst[:, t, h, :], vN[:, t, h * 512:(h + 1) * 512])
            link(last)
            for t in range(NT):
                last = v.bn_aggr(bnag[:, t, :], bnst[:, t, :, :])
            last.then_inc(sem["ln_var"], 1)
            weights(1)
            skip(1)
            exponents(3)
            dve.wait_ge(sem["ln_rms"], 1)
            link(v.reciprocal(stat[:, 6:8], stat[:, 8:10]))
            for t in range(NT):
                last = v.tensor_scalar(vN[:, t, :], vN[:, t, :], bnag[:, t, 0:1], stat[:, 6 + t:7 + t],
                                       ALU.subtract, ALU.mult)
            last.then_inc(sem["vn_ready"], 1)
            dve.wait_ge(sem["mult_ready"], 1)
            link(v.tensor_tensor(gxT, gxT, a2T, ALU.mult))
            dve.wait_ge(sem["a_ready"], 1)
            scans = list(range(KD))

            def scan(n):
                for j in scans[:n]:
                    v.tensor_tensor_scan(xaT[:, j, :], aT[:, j, :], gxT[:, j, :], 0.0, ALU.mult, ALU.add)
                del scans[:n]

            for i in range(2, KD):
                weights(i)
                scan(1)
                skip(i)
                if i + 2 < KD:
                    exponents(i + 2)
                if i == 6:
                    dve.wait_ge(read["u"], 4)
                    for g in range(SGU_G):
                        ps = take(f"sg{g}")
                        bias = sgub[:, g:g + 1, :].to_broadcast([P, NT, SGU_BLOCK])
                        for f in range(2):
                            half = ps[:, f * T:(f + 1) * T].rearrange("p (n t) -> p n t", n=NT)
                            last = v.scalar_tensor_tensor(out=half, in0=half, scalar=col("gsgu", 2 * g + f), in1=bias,
                                                          op0=ALU.mult, op1=ALU.add)
                        link(last)
                        v.tensor_tensor(uT[:, 2 * g:2 * g + 2, :], uT[:, 2 * g:2 * g + 2, :], halves(ps), ALU.mult
                                        ).then_inc(read["sg"], 1)
            v.tensor_tensor_scan(xaT[:, scans[0], :], aT[:, scans[0], :], gxT[:, scans[0], :], 0.0,
                                 ALU.mult, ALU.add)
            link(v.tensor_tensor_scan(xaT[:, scans[1], :], aT[:, scans[1], :], gxT[:, scans[1], :], 0.0,
                                      ALU.mult, ALU.add))
            dve.wait_ge(read["ya"], 4)
            v.tensor_tensor(xaT, xaT, yaT, ALU.mult).then_inc(sem["yA_ready"], 1)

            def merge(b, h):
                for i in (2 * h, 2 * h + 1):
                    s = slice(2 * i, 2 * i + 2)
                    n = "ABC"[b]
                    ps = take(f"p{n}{i}")
                    dve.wait_ge(read["g" + n], i + 1)
                    if b == 0:
                        v.tensor_tensor(mergedT[:, s, :], gateT[:, s, :], halves(ps), ALU.mult
                                        ).then_inc(read["pA"], 1)
                        continue
                    v.tensor_tensor(gateT[:, s, :], gateT[:, s, :], halves(ps), ALU.mult).then_inc(read["p" + n], 1)
                    dve.wait_ge(read["p" + n], i + 1)
                    v.tensor_tensor(mergedT[:, s, :], mergedT[:, s, :], gateT[:, s, :], ALU.add
                                    ).then_inc(sem["merged_" + n], 1)

            merge(0, 0)
            merge(0, 1)
            dve.wait_ge(read["cn"], 2)
            link(v.reciprocal(crms, crms))
            for f in range(KD):
                last = v.scalar_tensor_tensor(out=ycT[:, f, :], in0=ycT[:, f, :], scalar=col("gssm", f),
                                              in1=crms[:, f * GROUPS // KD, :], op0=ALU.mult, op1=ALU.mult)
            last.then_inc(sem["yC_ready"], 1)
            merge(1, 0)
            dve.wait_ge(sem["mem_rms"], 1)
            link(v.reciprocal(stat[:, 14:16], stat[:, 12:14]))
            for t in range(NT):
                v.tensor_scalar(memnN[:, t, :], memN[:, t, :], stat[:, 14 + t:15 + t], None, ALU.mult
                                ).then_inc(sem["memn_ready"], 1)
            merge(1, 1)
            for i in range(4):
                ps = take(f"mt{i}")
                for f in range(2):
                    last = v.tensor_scalar(memT[:, 2 * i + f, :], ps[:, f * T:(f + 1) * T], col("gmem", 2 * i + f),
                                           None, ALU.mult)
                last.then_inc(read["mt"], 1)
            merge(2, 0)
            merge(2, 1)

            def add_x(name):
                ps = take(name)
                s = slice(2 * member(name), 2 * member(name) + 2)
                v.tensor_tensor(xT[:, s, :], xT[:, s, :], halves(ps), ALU.add).then_inc(read[family(name)], 1)

            for i in range(4):
                add_x(f"wo{i}")
            dve.wait_ge(read["xn"], 1)
            link(v.reciprocal(x1rms, x1rms))
            for f in range(KD):
                v.scalar_tensor_tensor(out=hxT[:, f, :], in0=xT[:, f, :], scalar=col("gxa", f), in1=x1rms,
                                       op0=ALU.mult, op1=ALU.mult).then_inc(sem["hx_ready"], 1)
            for h in range(XA_HEADS + 1):
                if h < XA_HEADS:
                    ps = take(f"sc{h}")
                    c = slice(NT * h, NT * h + NT)
                    link(v.reduce_max(sm[:, 0, c], ps[:, :].rearrange("p (t m) -> p t m", t=NT), AX.X))
                    v.tensor_scalar(sm[:, 1, c], sm[:, 0, c], -1.0, None, ALU.mult).then_inc(sem["smax_ready"], 1)
                if h > 0:
                    c = slice(NT * (h - 1), NT * h)
                    dve.wait_ge(read["sc"], h)
                    link(v.reciprocal(sm[:, 3, c], sm[:, 2, c]))
                    for t in range(NT):
                        last = v.tensor_scalar(probs[:, h - 1, t, :], probs[:, h - 1, t, :],
                                               sm[:, 3, NT * (h - 1) + t:NT * (h - 1) + t + 1], None, ALU.mult)
                    last.then_inc(sem["p_ready"], 1)
            for h in range(XA_HEADS):
                ps = take(f"o{h}")
                v.tensor_copy(oT[:, 2 * h:2 * h + 2, :], halves(ps)).then_inc(read["o"], 1)
            for i in range(4):
                add_x(f"ao{i}")
            dve.wait_ge(sem["x2_rms"], 1)
            v.reciprocal(stat[:, 20:22], stat[:, 18:20]).then_inc(sem["x2_rinv"], 1)
            dve.wait_ge(sem["x2_rinv"], 1)
            ps = take("rt0")
            lf = rt2("l")
            for t in range(NT):
                last = v.scalar_tensor_tensor(out=lf[:, t, :], in0=ps[:, t * 64:t * 64 + NG + NE],
                                              scalar=stat[:, 20 + t:21 + t], in1=br[:, :], op0=ALU.mult, op1=ALU.add)
            last.then_inc(read["rt"], 1)
            dve.wait_ge(read["rt"], 1)
            gl = rt2("lg")
            v.tensor_copy(gl, lf[:, :, 0:NG])
            v.tensor_copy(rt2("le"), lf[:, :, NG:])
            link(v.tensor_scalar(rv("rev"), iota_f[:, 0:NE], -1.0, float(NE), ALU.mult, ALU.add))

            def wide(name, n):
                return rv(name).rearrange("p (t o) -> p t o", o=1).to_broadcast([P, NT, n])

            def first_hot(src, n, mx, hot):
                link(v.reduce_max(rv(mx), src, AX.X))
                eq = rv("eq")[:, 0:NT * n].rearrange("p (t n) -> p t n", t=NT)
                key = rv("key")[:, 0:NT * n].rearrange("p (t n) -> p t n", t=NT)
                link(v.tensor_tensor(eq, src, wide(mx, n), ALU.is_equal))
                rev = rv("rev")[:, 0:n].rearrange("p (o n) -> p o n", o=1).to_broadcast([P, NT, n])
                link(v.tensor_tensor(key, eq, rev, ALU.mult))
                link(v.reduce_max(rv("km"), key, AX.X))
                link(v.tensor_tensor(hot, key, wide("km", n), ALU.is_equal))

            first_hot(gl, NG, "mxg", rt2("gm"))
            v.tensor_tensor(rt2("dl"), gl, wide("mxg", NG), ALU.subtract).then_inc(sem["gexp_in"], 1)
            link(v.tensor_scalar(rv("gneg"), rv("gm"), BIG, -BIG, ALU.mult, ALU.add))
            em3 = rv("em").rearrange("p (g e) -> p g e", e=EPG)

            def over(name):
                return rv(name).rearrange("p (g o) -> p g o", o=1).to_broadcast([P, NT * NG, EPG])

            link(v.tensor_tensor(em3, rv("le").rearrange("p (g e) -> p g e", e=EPG), over("gm"), ALU.mult))
            link(v.tensor_tensor(em3, em3, over("gneg"), ALU.add))
            first_hot(rt2("em"), NE, "m1", rt2("o1"))
            link(v.scalar_tensor_tensor(out=rv("em"), in0=rv("o1"), scalar=-3 * BIG, in1=rv("em"),
                                        op0=ALU.mult, op1=ALU.add))
            first_hot(rt2("em"), NE, "m2", rt2("o2"))
            v.tensor_tensor(rv("as"), rv("o1"), rv("o2"), ALU.add).then_inc(sem["assign_ready"], 1)
            v.tensor_tensor(rv("dm"), rv("m2"), rv("m1"), ALU.subtract).then_inc(sem["texp_in"], 1)
            dve.wait_ge(sem["gexp_done"], 1)
            link(v.reduce_sum(rv("gs"), rt2("ge"), AX.X))
            link(v.reciprocal(rv("gs"), rv("gs")))
            dve.wait_ge(sem["texp_done"], 1)
            link(v.tensor_scalar(rv("w1"), rv("te"), 1.0, None, ALU.add))
            link(v.reciprocal(rv("w1"), rv("w1")))
            link(v.tensor_tensor(rv("w1"), rv("w1"), rv("gs"), ALU.mult))
            link(v.tensor_tensor(rv("w2"), rv("w1"), rv("te"), ALU.mult))
            ps = take("rk0")
            link(v.tensor_copy(rv("cnt"), ps[:, 2 * NE:3 * NE]))
            link(v.tensor_tensor_scan(rv("incl"), ones[:, 0:NE], rv("cnt"), 0.0, ALU.mult, ALU.add))
            link(v.tensor_tensor(rv("st"), rv("incl"), rv("cnt"), ALU.subtract))
            v.tensor_tensor(rt2("pos"), ps[:, 0:2 * NE].rearrange("p (t n) -> p t n", t=NT),
                            rv("st").rearrange("p (o n) -> p o n", o=1).to_broadcast([P, NT, NE]), ALU.add
                            ).then_inc(read["rk"], 1)
            dve.wait_ge(read["rk"], 1)
            for hot, p in (("o1", "p1"), ("o2", "p2")):
                link(v.tensor_tensor(rv("pp"), rv(hot), rv("pos"), ALU.mult))
                link(v.reduce_sum(rv(p), rt2("pp"), AX.X))
            for t in range(NT):
                last = v.tensor_scalar(sel[:, t, :], iota_f[:, :], rv("p1")[:, t:t + 1], None, ALU.is_equal)
            link(last)
            for t in range(NT):
                v.scalar_tensor_tensor(out=sel[:, t, :], in0=iota_f[:, :], scalar=rv("p2")[:, t:t + 1],
                                       in1=sel[:, t, :], op0=ALU.is_equal, op1=ALU.add).then_inc(sem["sel_ready"], 1)
            for t in range(NT):
                v.tensor_scalar(selw[:, t, :], iota_f[:, :], rv("p1")[:, t:t + 1], rv("w1")[:, t:t + 1],
                                ALU.is_equal, ALU.mult)
                link(v.tensor_scalar(seltmp, iota_f[:, :], rv("p2")[:, t:t + 1], rv("w2")[:, t:t + 1],
                                     ALU.is_equal, ALU.mult))
                v.tensor_tensor(selw[:, t, :], selw[:, t, :], seltmp, ALU.add).then_inc(sem["selw_ready"], 1)
                dve.wait_ge(sem["selw_ready"], t + 1)
            v.tensor_copy(starts_i[0:1, 0:NE], rv("st")[0:1, :])
            link(v.memset(starts_i[0:1, NE:NE + 1], 0))

            def ov(i, n=1):
                return ovf[0:1, i * NCAND:(i + n) * NCAND]

            st1, cnt1 = rv("st")[0:1, :], rv("cnt")[0:1, :]
            for j in range(1, T // WIN):
                c = slice((j - 1) * NE, j * NE)
                v.tensor_scalar(ov(0)[:, c], cnt1, float(WIN * j), None, ALU.is_gt)
                v.tensor_scalar(ov(1)[:, c], st1, float(WIN * j), None, ALU.add)
                v.tensor_scalar(ov(2)[:, c], rv("incl")[0:1, :], float(-WIN), None, ALU.add)
                last = v.tensor_copy(ov(3)[:, c], iota_f[0:1, 0:NE])
            link(last)
            link(v.memset(ov(5), 1.0))
            link(v.tensor_tensor(ov(1), ov(1), ov(2), ALU.min))
            link(v.tensor_tensor_scan(ov(4), ov(5), ov(0), 0.0, ALU.mult, ALU.add))
            link(v.tensor_tensor(ov(6), ov(4), ov(0), ALU.mult))
            big = ovf[0:1, 10 * NCAND:(10 + NOV) * NCAND].rearrange("p (o c) -> p o c", c=NCAND)
            big2 = ovf[0:1, (10 + NOV) * NCAND:(10 + 2 * NOV) * NCAND].rearrange("p (o c) -> p o c", c=NCAND)

            def each(i):
                return ov(i).rearrange("p (o c) -> p o c", o=1).to_broadcast([1, NOV, NCAND])

            place = iota_f[0:1, 1:NOV + 1].rearrange("p (o c) -> p o c", c=1).to_broadcast([1, NOV, NCAND])
            link(v.tensor_tensor(big, each(6), place, ALU.is_equal))
            link(v.tensor_tensor(big2, big, each(3), ALU.mult))
            link(v.reduce_sum(ov(7)[:, 1:NOV + 1], big2, AX.X))
            link(v.tensor_tensor(big2, big, each(1), ALU.mult))
            link(v.reduce_sum(ov(7)[:, NOV + 1:2 * NOV + 1], big2, AX.X))
            link(v.tensor_copy(ov(7)[:, 0:1], ov(4)[:, NCAND - 1:NCAND]))
            v.tensor_copy(ov_i[0:1, 0:2 * NOV + 1], ov(7)[:, 0:2 * NOV + 1]).then_inc(sem["ov_ready"], 1)

            dve.wait_ge(sem["ov_ready"], 1)
            dve.wait_ge(sem["pad_ready"], 1)

            def window(start, p):
                v.tensor_copy(xe[:, p], slotsT[:, :, bass.ds(start, WIN)]).then_inc(sem["xe_ready"], 1)

            def first_slot(e):
                return dve.value_load(starts_i[0:1, bass.ds(e, 1)], min_val=0, max_val=SLOTS)

            def hidden(n, p):
                dve.wait_ge(sem["esilu_ready"], n + 1)
                v.tensor_tensor(hm[:, p], sil[:, p], psum[4 * p][:, SEG:2 * SEG], ALU.mult).then_inc(sem["h_ready"], 1)

            def result(n, p, start):
                dve.wait_ge(sem["yturn_done"], n + 1)
                turned = psum[4 * p + 3][:, :].rearrange("p (j h w) -> p j h w", h=2, w=WIN)
                room = yT[:, :, bass.ds(start, WIN)].rearrange("p (h j) w -> p j h w", h=2)
                for h in range(2):
                    last = v.tensor_copy(room[:, :, h, :], turned[:, :, h, :])
                last.then_inc(sem["y_slots"], 1)

            first = first_slot(0)
            dve.wait_ge(read["ga"], KD)
            window(first, 0)
            with dve.Fori(0, NE // 2) as i:
                for p in range(2):
                    window(first_slot(i * 2 + (p + 1)), 1 - p)
                    hidden(i * 2 + p, p)
                    result(i * 2 + p, p, first_slot(i * 2 + p))
            n_ov = dve.value_load(ov_i[0:1, 0:1], min_val=0, max_val=NOV)
            with dve.If(n_ov > 0):
                with dve.Fori(0, n_ov) as o:
                    s = dve.value_load(ov_i[0:1, bass.ds(o + (NOV + 1), 1)], min_val=0, max_val=SLOTS)
                    window(s, 1)
                    hidden(o + NE, 0)
                    result(o + NE, 0, s)
            v.tensor_copy(stat[:, 30:31], epsc[:]).then_inc(sem["y_complete"], 1)
            for n in range(SLOTS // P):
                dve.wait_ge(sem["ysn_ready"], 2 * n + 2)
                v.tensor_copy(ySN[:, n, 512:D], psum[2 * n + 1][:, :]).then_inc(sem["ySNb_ready"], 1)
            dve.wait_ge(sem["gfin_loaded"], 16)
            for t in range(NT):
                for h in range(2):
                    i = 2 * t + h
                    c = slice(h * 512, (h + 1) * 512)
                    dve.wait_ge(sem["fin_done"], i + 1)
                    v.tensor_tensor(x2N[:, t, c], x2N[:, t, c], psum[i][:, :], ALU.add).then_inc(sem["x3_ready"], 1)
                dve.wait_ge(sem["x3sq_ready"], t + 1)
                v.tensor_tensor(stat[:, 22 + t:23 + t], sq3[:, 2 * t:2 * t + 1], sq3[:, 2 * t + 1:2 * t + 2], ALU.add
                                ).then_inc(sem["x3sum_ready"], 1)
                dve.wait_ge(sem["x3_rms"], t + 1)
                link(v.reciprocal(stat[:, 26 + t:27 + t], stat[:, 24 + t:25 + t]))
                for h in range(2):
                    c = slice(h * 512, (h + 1) * 512)
                    v.scalar_tensor_tensor(out=outN[:, t, c], in0=x2N[:, t, c], scalar=stat[:, 26 + t:27 + t],
                                           in1=gfin[:, c], op0=ALU.mult, op1=ALU.mult).then_inc(sem["o_final"], 1)

        @block_.tensor
        def _(pe):
            mm, tp = nc.tensor.matmul, nc.tensor.transpose
            count = [0]

            def begin(name):
                assert order[count[0]] == name
                if count[0] >= NB:
                    last = order[count[0] - NB]
                    pe.wait_ge(read[family(last)], member(last) + 1)
                count[0] += 1
                return bank(name)

            def end(ins):
                ins.then_inc(sem["unit_done"], 1)

            def slab_of(n):
                pe.wait_ge(filled[n % PRE], 16 * (n // PRE + 1))
                return ring[:, n % PRE, :].rearrange("p (k n) -> p k n", k=KD)

            def dense(name, src):
                i = member(name)
                first = name if i % 2 else family(name) + str(i + 1)
                w = slab_of(SLAB_OF[first])
                ps = begin(name)
                for f in range(2):
                    c = (2 * (i % 2) + f) * P
                    for k in range(KD):
                        last = mm(ps[:, f * T:(f + 1) * T], w[:, k, c:c + P], src[:, k, :],
                                  start=k == 0, stop=k == KD - 1)
                end(last)

            def dense_rows(name, src):
                i = member(name)
                first = name if i % 2 else family(name) + str(i + 1)
                w = slab_of(SLAB_OF[first])
                ps = begin(name)
                t = i % 2
                for k in range(KD):
                    last = mm(ps[:, :], src[:, k, t * P:(t + 1) * P], w[:, k, :], start=k == 0, stop=k == KD - 1)
                end(last)

            def to_T(name, src):
                ps = begin(name)
                i = TILEPAIR[name]
                for f in range(2):
                    for t in range(NT):
                        last = tp(ps[:, f * T + t * P:f * T + (t + 1) * P],
                                  src[:, t, (2 * i + f) * P:(2 * i + f + 1) * P], ident[:])
                end(last)

            def to_N(name, t, tile, h):
                ps = begin(name)
                for f in range(4):
                    last = tp(ps[:, f * P:(f + 1) * P], tile(4 * h + f)[:, t * P:(t + 1) * P], ident[:])
                end(last)

            TILEPAIR = {"ha0": 0, "hb0": 1, "ha1": 2, "hb1": 3}
            for i in range(4):
                TILEPAIR[f"xt{i}"] = TILEPAIR[f"mt{i}"] = i

            pe.wait_ge(sem["consts"], 1)
            pe.wait_ge(sem["xn_ready"], NT)
            for name in ("ha0", "hb0", "ha1", "hb1"):
                to_T(name, xnN)
            pe.wait_ge(sem["par_loaded"], 16 * len(rows))
            for i in range(2):
                ps = begin(f"par{i}")
                n = min(P, npar - i * P)
                end(tp(ps[:, 0:n], prow[0:n, i, :], ident[0:n, 0:n]))
            pe.wait_ge(read["ha"], 2)
            pe.wait_ge(read["hb"], 2)
            for i in range(8):
                dense(f"xbc{i}", hT)
                if i == 1:
                    pe.wait_ge(sem["small_loaded"], 16 * len(small))
                    ps = begin("dt0")
                    for t in range(NT):
                        for k in range(KD):
                            last = mm(ps[:, t * HEADS:(t + 1) * HEADS], hT[:, k, t * P:(t + 1) * P], wdt[:, k, :],
                                      start=k == 0, stop=k == KD - 1)
                    end(last)
            for i in range(4):
                dense(f"xa{i}", hT)
            pe.wait_ge(sem["dta_ready"], 1)
            dta = dtw[:, 6, :].rearrange("p (t h) -> p t h", t=NT)
            ps = begin("cs0")
            mm(ps[:, 0:HEADS], mask[:, 0:P], dta[:, 0, :], start=True, stop=True)
            mm(ps[:, HEADS:2 * HEADS], ones[:], dta[:, 0, :], start=True, stop=False)
            end(mm(ps[:, HEADS:2 * HEADS], mask[:, 0:P], dta[:, 1, :], start=False, stop=True))
            for i in range(4):
                to_T(f"xt{i}", xN)
            for i in range(2):
                dense(f"z{i}", hT)
            pe.wait_ge(sem["silu_ready"], XBC_TILES // 2)
            for i in range(4):
                to_N(f"xs{i}", i // 2, xbcT, i % 2)
            for i in range(2, 4):
                dense(f"z{i}", hT)
            for g in range(GROUPS):
                ps = begin(f"cb{g}")
                bT, cT = xbcT(KD + g), xbcT(KD + GROUPS + g)
                mm(ps[:, 0:T], bT[:, 0:P], cT, start=True, stop=True)
                end(mm(ps[:, T:3 * P], bT[:, P:T], cT[:, P:T], start=True, stop=True))
            pe.wait_ge(read["xa"], 4)
            pe.wait_ge(read["xt"], 4)
            for i in range(4):
                dense_rows(f"v{i}", hT)
                for j in (2 * i, 2 * i + 1):
                    ps = begin(f"lg{j}")
                    mm(ps[:, 0:T], gxw[:, j, :], xaT[:, j, :], start=True, stop=True)
                    end(mm(ps[:, T:2 * T], gaw[:, j, :], xaT[:, j, :], start=True, stop=True))
            ps = begin("wst0")
            for g in range(SGU_G):
                last = tp(ps[:, g * P:(g + 1) * P], sguw[:, g, :], ident[:])
            end(last)

            def cum(i):
                ps = begin(f"r{i}")
                for h in range(2):
                    hd = 2 * i + h
                    mm(ps[:, h * T:(h + 1) * T], dta[:, 0, hd:hd + 1].to_broadcast([P, P]), mask[:, 0:T],
                       start=True, stop=False)
                    last = mm(ps[:, h * T + P:(h + 1) * T], dta[:, 1, hd:hd + 1].to_broadcast([P, P]), mask[:, 0:P],
                              start=False, stop=True)
                end(last)

            def heads(i):
                pe.wait_ge(sem["w_ready"], i + 1)
                ps = begin(f"y{i}")
                for h in range(2):
                    hd = 2 * i + h
                    o = ps[h * HD:(h + 1) * HD, :]
                    mm(o[:, 0:T], xsN[:, 0, hd * HD:(hd + 1) * HD], dec[:, i % 2, h, 0:T], start=True, stop=False)
                    last = mm(o[:, P:T], xsN[:, 1, hd * HD:(hd + 1) * HD], dec[:, i % 2, h, T:], start=False, stop=True)
                end(last)

            pe.wait_ge(read["xs"], 4)
            dense("u0", hT)
            cum(0)
            cum(1)
            for i in range(1, 4):
                dense(f"u{i}", hT)
                heads(i - 1)
                cum(i + 1)
            for i in range(3):
                dense(f"ya{i}", hT)
                heads(3 + i)
                cum(5 + i)
            dense("ya3", hT)
            heads(6)
            pe.wait_ge(sem["vn_ready"], 1)
            pe.wait_ge(read["wst"], 1)
            for g in range(SGU_G):
                ps = begin(f"sg{g}")
                for f in range(2):
                    for n in range(NT):
                        last = mm(ps[:, f * T + n * P:f * T + (n + 1) * P], vN[:, n, (2 * g + f) * P:(2 * g + f + 1) * P],
                                  sguwT[:, g, :], start=True, stop=True)
                end(last)
            heads(7)

            def branch(b, src, ready, n):
                for h in range(2):
                    for i in (2 * h, 2 * h + 1):
                        dense(f"g{b}{i}", hT)
                    pe.wait_ge(ready, n)
                    for i in (2 * h, 2 * h + 1):
                        dense(f"p{b}{i}", src)

            branch("A", xaT, sem["yA_ready"], 1)
            pe.wait_ge(sem["csq_ready"], 1)
            for i in range(2):
                ps = begin(f"cn{i}")
                for g in range(2):
                    for f in range(2):
                        last = mm(ps[:, g * T:(g + 1) * T], onesm[:], csq[:, 4 * i + 2 * g + f, :],
                                  start=f == 0, stop=f == 1)
                end(last)
            branch("B", uT, read["sg"], SGU_G)
            pe.wait_ge(sem["memn_ready"], NT)
            for i in range(4):
                to_T(f"mt{i}", memnN)
            branch("C", ycT, sem["yC_ready"], 1)
            pe.wait_ge(sem["merged_C"], 4)
            for i in range(4):
                dense(f"wo{i}", mergedT)
            pe.wait_ge(read["mt"], 4)
            for i in range(2):
                dense(f"k{i}", memT)
            pe.wait_ge(sem["x1sq_ready"], 4)
            ps = begin("xn0")
            for k in range(KD):
                last = mm(ps[:, 0:T], onesm[:], x1sq[:, k, :], start=k == 0, stop=k == KD - 1)
            end(last)
            for i in range(2, 4):
                dense(f"k{i}", memT)
            pe.wait_ge(sem["hx_ready"], KD)
            for i in range(4):
                dense(f"q{i}", hxT)
            pe.wait_ge(read["q"], 4)
            pe.wait_ge(read["k"], 4)
            for h in range(XA_HEADS):
                ps = begin(f"sc{h}")
                for t in range(NT):
                    for j in range(2):
                        last = mm(ps[:, t * T:(t + 1) * T], QT[:, 2 * h + j, t * P:(t + 1) * P], KT[:, 2 * h + j, :],
                                  start=j == 0, stop=j == 1)
                end(last)
            for i in range(4):
                dense_rows(f"va{i}", memT)

            def turn(h):
                pe.wait_ge(sem["p_ready"], h + 1)
                ps = begin(f"pt{h}")
                for j in range(NT):
                    for t in range(NT):
                        last = tp(ps[:, j * T + t * P:j * T + (t + 1) * P], probs[:, h, t, j * P:(j + 1) * P], ident[:])
                end(last)

            def attend(h):
                pe.wait_ge(read["pt"], h + 1)
                ps = begin(f"o{h}")
                for f in range(2):
                    for j in range(NT):
                        last = mm(ps[:, f * T:(f + 1) * T], VN[:, j, (2 * h + f) * P:(2 * h + f + 1) * P],
                                  probsT[:, h, j, :], start=j == 0, stop=j == NT - 1)
                end(last)

            turn(0)
            pe.wait_ge(read["va"], 4)
            for h in range(1, XA_HEADS):
                turn(h)
                attend(h - 1)
            attend(XA_HEADS - 1)
            pe.wait_ge(read["o"], 4)
            for i in range(4):
                dense(f"ao{i}", oT)
            pe.wait_ge(read["ao"], 4)
            pe.wait_ge(sem["wr_ready"], 1)
            ps = begin("rt0")
            for t in range(NT):
                for k in range(KD):
                    mm(ps[:, t * 64:t * 64 + NG + NE], xT[:, k, t * P:(t + 1) * P], wr[:, k, :],
                       start=k == 0, stop=k == KD - 1)
            pe.wait_ge(sem["x2sq_ready"], 4)
            for t in range(NT):
                for k in range(KD):
                    last = mm(ps[:, 128 + t:129 + t], x2sq[:, k, t * P:(t + 1) * P], ones[:, 0:1],
                              start=k == 0, stop=k == KD - 1)
            end(last)
            for i in range(4):
                to_N(f"tr{i}", i % 2, lambda f: xT[:, f, :], i // 2)
            pe.wait_ge(sem["assign_ready"], 1)
            asg = rt2("as")
            ps = begin("rk0")
            mm(ps[:, 0:NE], strict[:], asg[:, 0, :], start=True, stop=True)
            mm(ps[:, NE:2 * NE], ones[:], asg[:, 0, :], start=True, stop=False)
            mm(ps[:, NE:2 * NE], strict[:], asg[:, 1, :], start=False, stop=True)
            mm(ps[:, 2 * NE:3 * NE], ones[:], asg[:, 0, :], start=True, stop=False)
            end(mm(ps[:, 2 * NE:3 * NE], ones[:], asg[:, 1, :], start=False, stop=True))
            pe.wait_ge(sem["sel_ready"], NT)
            pe.wait_ge(sem["h3_ready"], 1)
            for k in range(KD):
                ps = begin(f"ga{k}")
                for t in range(NT):
                    last = mm(ps[:, :], h3N[:, t, k * P:(k + 1) * P], sel[:, t, :], start=t == 0, stop=t == NT - 1)
                end(last)
            pe.wait_ge(sem["selw_ready"], NT)
            for i in range(2):
                ps = begin(f"st{i}")
                for s in range(2):
                    for t in range(NT):
                        last = tp(ps[:, s * T + t * P:s * T + (t + 1) * P],
                                  selw[:, t, (2 * i + s) * P:(2 * i + s + 1) * P], ident[:])
                end(last)
            assert count[0] == len(order)
            for name in order[-NB:]:
                pe.wait_ge(read[family(name)], member(name) + 1)

            def ffn(n, p, s0, xin, arrived):
                pe.wait_ge(sem["xe_ready"], n + 1 + (xin != p))
                for j in range(2):
                    pe.wait_ge(filled[s0 + j], arrived(s0))
                    w = ring[:, s0 + j, :].rearrange("p (k g n) -> p k g n", k=4, g=2)
                    for k in range(4):
                        for c in range(2):
                            last = mm(psum[4 * p][c * WIN:(c + 1) * WIN, :], xe[:, xin, 4 * j + k, :],
                                      w[:, k, :, c * SEG:(c + 1) * SEG], start=4 * j + k == 0, stop=4 * j + k == KD - 1)
                    last.then_inc(sem["half_done" if j == 0 else "gu_done"], 1)
                pe.wait_ge(sem["h_ready"], n + 1)
                for j in range(SEG // P):
                    last = tp(psum[4 * p + 1][:, j * P:(j + 1) * P], hm[:, p, j * P:(j + 1) * P], ident[:])
                last.then_inc(sem["turn_done"], 1)
                pe.wait_ge(filled[s0 + 2], arrived(s0))
                pe.wait_ge(sem["hT_ready"], n + 1)
                w = ring[:, s0 + 2, :].rearrange("p (k n) -> p k n", k=NF)
                for k in range(NF):
                    c, j = k // (SEG // P), k % (SEG // P)
                    for h in range(2):
                        last = mm(psum[4 * p + 2][h * WIN:(h + 1) * WIN, :], hmT[:, p, j, c * WIN:(c + 1) * WIN],
                                  w[:, k, h * 512:(h + 1) * 512], start=k == 0, stop=k == NF - 1)
                last.then_inc(sem["dn_done"], 1)
                pe.wait_ge(sem["yS_ready"], n + 1)
                for j in range(4):
                    last = tp(psum[4 * p + 3][:, j * P:(j + 1) * P], yS[:, j * P:(j + 1) * P], ident[:])
                last.then_inc(sem["yturn_done"], 1)

            with pe.Fori(0, NE // 2) as i:
                for p in range(2):
                    ffn(i * 2 + p, p, PRE * p, p, lambda s0: (i + 1 + (0 if s0 else PREFILLS)) * 16)
            pe.wait_ge(sem["ov_ready"], 1)
            n_ov = pe.value_load(ov_i[0:1, 0:1], min_val=0, max_val=NOV)
            with pe.If(n_ov > 0):
                with pe.Fori(0, n_ov) as o:
                    ffn(o + NE, 0, 0, 1, lambda s0: (o + (PREFILLS + NE // 2 + 1)) * 16)
            pe.wait_ge(sem["y_complete"], 1)
            for s in range(SLOTS // P):
                for h in range(2):
                    for f in range(4):
                        last = tp(psum[2 * s + h][:, f * P:(f + 1) * P], yT[:, 4 * h + f, s * P:(s + 1) * P], ident[:])
                    last.then_inc(sem["ysn_ready"], 1)
            for t in range(NT):
                for h in range(2):
                    for s in range(SLOTS // P):
                        if t == 0:
                            pe.wait_ge(sem["ySNb_ready" if h else "ySNa_ready"], s + 1)
                        last = mm(psum[2 * t + h][:, :], scat[:, s, t * P:(t + 1) * P], ySN[:, s, h * 512:(h + 1) * 512],
                                  start=s == 0, stop=s == SLOTS // P - 1)
                    last.then_inc(sem["fin_done"], 1)


_INS = ['x', 'mem', 'norm_mix', 'w_in', 'conv_a_w', 'conv_a_b', 'lru_gx_w', 'lru_gx_b', 'lru_ga_w',
        'lru_ga_b', 'lru_lambda', 'sgu_norm', 'sgu_w', 'sgu_b', 'conv_c_w', 'conv_c_b', 'ssm_dt_bias',
        'ssm_a_log', 'ssm_d', 'ssm_norm', 'w_a_proj', 'w_b_proj', 'w_c_proj', 'w_out', 'norm_xa',
        'norm_mem', 'w_q', 'w_kv', 'w_o', 'norm_ffn', 'w_router_group', 'b_router_group',
        'w_router_expert', 'b_router_expert', 'w_gate_up', 'w_down', 'norm_final']
_OUTS = [((1, 256, 1024), 'float32')]


def kernel(**inputs):
    import numpy as _np
    import concourse.bacc as _bacc
    from concourse import mybir as _mybir
    from concourse.bass_utils import run_bass_kernel_spmd as _run

    nc = _bacc.Bacc("TRN2", target_bir_lowering=False, num_devices=1)
    arrays, args = {}, []
    for name in _INS:
        a = _np.ascontiguousarray(inputs[name])
        arrays[f"in_{name}_dram"] = a
        args.append(nc.dram_tensor(f"in_{name}_dram", a.shape, _mybir.dt.from_np(a.dtype), kind="ExternalInput").ap())
    for i, (shape, dtype) in enumerate(_OUTS):
        dt = _mybir.dt.from_np(_np.dtype(dtype))
        args.append(nc.dram_tensor(f"out_{i}_dram", shape, dt, kind="ExternalOutput").ap())
    encoder_kernel(nc, *args)
    r = _run(nc, [arrays], core_ids=[0])
    return r.results[0]["out_0_dram"]
```

```python
import concourse.bass as bass
from concourse import mybir
from contextlib import ExitStack

P = 128


def encoder_kernel(nc, x, mem, norm_mix, w_in, conv_a_w, conv_a_b, lru_gx_w, lru_gx_b, lru_ga_w,
                   lru_ga_b, lru_lambda, sgu_norm, sgu_w, sgu_b, conv_c_w, conv_c_b, ssm_dt_bias,
                   ssm_a_log, ssm_d, ssm_norm, w_a_proj, w_b_proj, w_c_proj, w_out, norm_xa,
                   norm_mem, w_q, w_kv, w_o, norm_ffn, w_router_group, b_router_group,
                   w_router_expert, b_router_expert, w_gate_up, w_down, norm_final, out):
    F32, I32 = mybir.dt.float32, mybir.dt.int32
    ALU, ACT, AX = mybir.AluOpType, mybir.ActivationFunctionType, mybir.AxisListType

    T = x.shape[1]
    D = x.shape[2]
    KD = D // P
    NT = T // P
    EPS = 1e-6
    CONV = conv_a_w.shape[1]
    HEADS = ssm_d.shape[1]
    GROUPS = 4
    HPG = HEADS // GROUPS
    HD = D // HEADS
    XBC_TILES = conv_c_w.shape[2] // P
    OFF_YA, OFF_UV = D, 2 * D
    OFF_Z = OFF_UV + 2 * D
    OFF_XBC = OFF_Z + D
    OFF_DT = OFF_XBC + XBC_TILES * P
    OFF_GATE = OFF_DT + HEADS
    SGU_BLOCK = sgu_w.shape[2]
    SGU_G = sgu_w.shape[1]
    CHUNK = 64
    LRU_C = 8.0
    XA_HEADS = 4
    XA_DH = D // XA_HEADS
    NG, NE = w_router_group.shape[2], w_router_expert.shape[2]
    EPG = NE // NG
    DE = w_down.shape[2]
    WIN = 64
    SLOTS = 2 * T
    SLOTP = SLOTS + WIN
    NOV = SLOTS // WIN - 1
    BIG = 1e30

    order = ["ha0", "hb0", "par0", "par1", "ha1", "hb1"]
    order += ["xbc0", "xbc1", "dt0"] + [f"xbc{i}" for i in range(2, 8)] + [f"xa{i}" for i in range(4)]
    order += ["cs0"] + [f"xt{i}" for i in range(4)]
    order += ["z0", "z1"] + [f"xs{i}" for i in range(4)] + ["z2", "z3"] + [f"cb{i}" for i in range(GROUPS)]
    for i in range(4):
        order += [f"v{i}", f"lg{2 * i}", f"lg{2 * i + 1}"]
    order += ["wst0", "u0", "r0", "r1", "u1", "y0", "r2", "u2", "y1", "r3", "u3", "y2", "r4",
              "ya0", "y3", "r5", "ya1", "y4", "r6", "ya2", "y5", "r7", "ya3", "y6"]
    order += [f"sg{i}" for i in range(4)] + ["y7"]
    for b in "ABC":
        for h in (0, 2):
            order += [f"g{b}{h}", f"g{b}{h + 1}", f"p{b}{h}", f"p{b}{h + 1}"]
        if b == "A":
            order += ["cn0", "cn1"]
        if b == "B":
            order += [f"mt{i}" for i in range(4)]
    order += [f"wo{i}" for i in range(4)] + ["k0", "k1", "xn0", "k2", "k3"]
    order += [f"q{i}" for i in range(4)] + [f"sc{i}" for i in range(4)] + [f"va{i}" for i in range(4)]
    order += ["pt0", "pt1", "o0", "pt2", "o1", "pt3", "o2", "o3"]
    order += [f"ao{i}" for i in range(4)] + ["rt0"] + [f"tr{i}" for i in range(4)] + ["rk0"]
    order += [f"ga{i}" for i in range(KD)] 
    U = {name: i for i, name in enumerate(order)}
    NB = 8
    RK, SELB = U["rk0"], 4
    BANK = [i % NB if i < RK else (i - RK) % SELB for i in range(len(order))]
    USED = ("half_done", "gu_done", "dn_done")

    def family(name):
        return name.rstrip("0123456789")

    def member(name):
        return int(name[len(family(name)):])

    SLABS = [(w_in, OFF_XBC + 512 * i, f"xbc{2 * i + 1}") for i in range(4)]
    SLABS += [(w_in, 512 * i, f"xa{2 * i + 1}") for i in range(2)]
    SLABS += [(w_in, OFF_Z + 512 * i, f"z{2 * i + 1}") for i in range(2)]
    SLABS += [(w_in, OFF_UV + D + 512 * i, f"v{2 * i + 1}") for i in range(2)]
    SLABS += [(w_in, OFF_UV + 512 * i, f"u{2 * i + 1}") for i in range(2)]
    SLABS += [(w_in, OFF_YA + 512 * i, f"ya{2 * i + 1}") for i in range(2)]
    for b, w in enumerate((w_a_proj, w_b_proj, w_c_proj)):
        for h in range(2):
            SLABS += [(w_in, OFF_GATE + b * D + 512 * h, f"g{'ABC'[b]}{2 * h + 1}"),
                      (w, 512 * h, f"p{'ABC'[b]}{2 * h + 1}")]
    for w, c0, name in ((w_out, 0, "wo"), (w_kv, 0, "k"), (w_q, 0, "q"), (w_kv, D, "va"), (w_o, 0, "ao")):
        SLABS += [(w, c0 + 512 * h, f"{name}{2 * h + 1}") for h in range(2)]
    NSLAB = len(SLABS)
    SLAB_OF = {last: n for n, (_, _, last) in enumerate(SLABS)}
    PRE = 3
    RING = 8
    PARTS = 3
    CYCLE = 8
    assert PARTS * CYCLE % RING == 0 and NE % CYCLE == 0 and CYCLE % 2 == 0
    PREFILLS = NSLAB // PRE
    assert NSLAB % PRE == 0

    ctx = ExitStack()
    with ctx:
        def sb(name, shape, dt=F32):
            return ctx.enter_context(nc.sbuf_tensor(name, shape, dt))

        ring = sb("ring", [P, 6, KD * 512])
        params = sb("params", [P, KD * 512])
        blk = sb("blk", [P, 9, KD * T])

        def block(i):
            if i < 9:
                return blk[:, i, :]
            return ring[:, PRE + (i - 9) // 2, (i - 9) % 2 * 2048:(i - 9) % 2 * 2048 + 2048]

        def slot(n):
            if n < 6:
                return ring[:, n, :]
            return blk[:, 7:9, :].rearrange("p b n -> p (b n)") if n == 6 else params[:, :]

        def asT(i):
            return block(i).rearrange("p (f t) -> p f t", t=T)

        def asN(i):
            return block(i).rearrange("p (t f) -> p t f", t=NT)

        hT, hxT = asT(0), asT(0)
        xT = asT(1)
        xN, vN, memT, x2N = asN(2), asN(2), asT(2), asN(2)
        xnN, xaT, memnN = asN(3), asT(3), asN(3)
        uT, KT = asT(4), asT(4)
        yaT, memN, VN = asT(5), asN(5), asN(5)
        junk, a2T, mergedT, oT, outN = asN(6), asT(6), asT(6), asT(6), asN(6)
        gateT, QT = asT(7), asT(7)
        ycT, x1sq, x2sq = asT(8), asT(8), asT(8)
        h3N = asN(6)
        xsN, zT, gxT, aT, csq = asN(11), asT(12), asT(13), asT(14), asT(13)

        def xbcT(f):
            return asT(9 + f // KD)[:, f % KD, :]

        probs = block(3).rearrange("p (h t m) -> p h t m", h=XA_HEADS, t=NT)
        probsT = block(8).rearrange("p (h j t) -> p h j t", h=XA_HEADS, j=NT)
        sel = block(0)[:, 0:NT * SLOTS].rearrange("p (t s) -> p t s", t=NT)
        slotsT = blk[:, 3:6, :].rearrange("p b n -> p (b n)")[:, 0:KD * SLOTP].rearrange("p (k s) -> p k s", k=KD)
        junk3 = asN(2)
        placed = blk[:, 1, 0:4 * NT * WIN].rearrange("p (b t d w) -> p b t d w", b=2, t=NT, d=2)
        scat = blk[:, 1, 4 * NT * WIN:4 * NT * WIN + 2 * T].rearrange("p (b t) -> p b t", b=2)
        chosen = blk[:, 0, 1536:1536 + 4 * NT].rearrange("p (b a) -> p b a", b=2)
        pw = blk[:, 0, 1600:1600 + 2 * NT * (NE + 1)].rearrange("p (a n) -> p a n", a=2 * NT)
        xe = blk[:, 1, 1024:2048].rearrange("p (b k w) -> p b k w", b=2, w=WIN)

        ident = sb("ident", [P, P])
        ones = sb("ones", [P, P])
        onesm = sb("onesm", [P, P])
        mask = sb("mask", [P, 3 * P])
        strict = sb("strict", [P, P])
        iota_i = blk[:, 8, 0:SLOTP].bitcast(I32)
        iota_f = sb("iota_f", [P, SLOTP])
        epsc = sb("epsc", [P, 1])
        zeros = sb("zeros", [P, P], mybir.dt.bfloat16)
        prow = sb("prow", [P, 2, P])
        par = sb("par", [P, 2, P])
        wdt = sb("wdt", [P, KD, HEADS])
        wr = sb("wr", [P, KD, NG + NE])
        br = sb("br", [P, NG + NE])
        gxw = params[:, 0:KD * P].rearrange("p (k n) -> p k n", k=KD)
        gaw = params[:, KD * P:2 * KD * P].rearrange("p (k n) -> p k n", k=KD)
        sguw, sguwT, sgub = (params[:, (2 * KD + SGU_G * i) * P:(2 * KD + SGU_G * (i + 1)) * P]
                             .rearrange("p (g n) -> p g n", g=SGU_G) for i in range(3))
        dtb = sb("dtb", [P, HEADS])
        alog = sb("alog", [P, HEADS])
        dsk = sb("dsk", [P, HEADS])
        dcol = sb("dcol", [P, KD])
        stat = sb("stat", [P, 32])
        c8 = sb("c8", [P, 6, KD])
        dtw = sb("dtw", [P, 7, NT * HEADS])
        csN = sb("csN", [P, NT, HEADS])
        cbm = sb("cbm", [P, GROUPS, 3 * P])
        dec = sb("dec", [P, 2, 2, 3 * P])
        bnst = sb("bnst", [P, NT, 2, 6])
        bnag = sb("bnag", [P, NT, 2])
        sq3 = sb("sq3", [P, 2 * NT])
        sm = sb("sm", [P, 4, XA_HEADS * NT])
        decflat = dec[:, :, :, :].rearrange("p a b c -> p (a b c)")
        crms = decflat[:, 0:GROUPS * T].rearrange("p (g t) -> p g t", t=T)
        x1rms = decflat[:, GROUPS * T:(GROUPS + 1) * T]
        gfin = decflat[:, 0:D]
        cflat = cbm[:, :, :].rearrange("p g c -> p (g c)")
        NF = DE // P
        SEG = DE // 2
        sil = cflat[:, 0:2 * SEG].rearrange("p (b f) -> p b f", b=2)
        hm = cflat[:, 2 * SEG:4 * SEG].rearrange("p (b f) -> p b f", b=2)
        hmT = cflat[:, 4 * SEG:6 * SEG].rearrange("p (b j c) -> p b j c", b=2, c=P)
        yS = decflat[:, D:D + 512]
        NCAND = (T // WIN - 1) * NE
        ovf = cflat[0:1, 0:(8 + NOV) * NCAND]
        ovf2 = blk[0:1, 1, 1024:1024 + NOV * NCAND]
        starts_i = sb("starts_i", [1, NE + 1], I32)
        ov_i = sb("ov_i", [1, 2 * NOV + 2], I32)

        psum = [ctx.enter_context(nc.psum_tensor(f"bank{i}", [P, 512], F32)) for i in range(NB)]

        def bank(name):
            return psum[BANK[U[name]]]

        def gu_bank(p):
            return psum[p]

        turn_bank, down_bank = psum[2], psum[3]
        x3_bank = psum[4:8]

        def sems(names):
            return {n: ctx.enter_context(nc.semaphore(n)) for n in names.split()}

        sem = sems("""eps x_loaded par_loaded small_loaded late_loaded mem_loaded gfin_loaded out_stored fills consts
            act_step dve_step unit_done x_rms xn_ready
            conv_init silu_ready lam_ln alog_exp dt_ready dt_act dta_ready d_ready c_ready
            ln_var ln_rms vn_ready a2_ready a_ready a2_min mult_ready yA_ready
            exp_ready w_ready yz_ready csq_ready  yC_ready merged_B merged_C
            mem_rms memn_ready x1sq_ready hx_ready smax_ready p_ready
            wr_ready x2sq_ready x2_rms x2_rinv h3_ready gexp_in gexp_done texp_in texp_done assign_ready sel_ready
             ov_ready pad_ready half_done gu_done turn_done dn_done xe_ready chosen_ready placed_ready
            esilu_ready scat_ready h_ready hT_ready yS_ready x3_done x3sq_ready x3sum_ready x3_rms o_final""")
        read = {f: ctx.enter_context(nc.semaphore(f + "_read"))
                for f in sorted({family(n) for n in order})}
        filled = [ctx.enter_context(nc.semaphore(f"slot_filled{i}")) for i in range(RING)]

        def tiles(vector):
            return vector.rearrange("(f p) -> f p", p=P)

        rows, pcol, npar = [], {}, 0
        for name, ap, n in (("ccw", conv_c_w[0].rearrange("k (f p) -> (k f) p", p=P), CONV * XBC_TILES),
                            ("ccb", tiles(conv_c_b[0]), XBC_TILES),
                            ("caw", conv_a_w[0].rearrange("k (f p) -> (k f) p", p=P), CONV * KD),
                            ("cab", tiles(conv_a_b[0]), KD), ("gmix", tiles(norm_mix[0]), KD),
                            ("gxb", lru_gx_b[0], KD), ("gab", lru_ga_b[0], KD),
                            ("lam", tiles(lru_lambda[0]), KD), ("gsgu", tiles(sgu_norm[0]), KD),
                            ("gssm", tiles(ssm_norm[0]), KD), ("gxa", tiles(norm_xa[0]), KD),
                            ("gmem", tiles(norm_mem[0]), KD), ("gffn", tiles(norm_ffn[0]), KD)):
            assert npar // P == (npar + n - 1) // P
            rows.append((npar // P, npar % P, ap, n))
            pcol[name] = npar
            npar += n

        def col(name, i=0):
            c = pcol[name] + i
            return par[:, c // P, c % P:c % P + 1]

        def cols(name, n):
            c = pcol[name]
            return par[:, c // P, c % P:c % P + n]

        SOON = 4

        def spread(ap):
            return ap.partition_broadcast(P)

        small = [(wdt[:], w_in[0].rearrange("(k p) n -> p k n", p=P)[:, :, OFF_DT:OFF_DT + HEADS]),
                 (dtb[:], spread(ssm_dt_bias[0])), (alog[:], spread(ssm_a_log[0])), (dsk[:], spread(ssm_d[0])),
                 (gxw, lru_gx_w[0].rearrange("h i j -> i h j")), (gaw, lru_ga_w[0].rearrange("h i j -> i h j")),
                 (sguw, sgu_w[0].rearrange("g t s -> t g s")), (sgub, spread(sgu_b[0])),
                 (wr[:, :, 0:NG], w_router_group[0].rearrange("(k p) n -> p k n", p=P)),
                 (wr[:, :, NG:], w_router_expert[0].rearrange("(k p) n -> p k n", p=P)),
                 (br[:, 0:NG], spread(b_router_group[0])), (br[:, NG:], spread(b_router_expert[0]))]

        rtl, used = {}, 0
        for name, n in (("l", NT * (NG + NE)), ("lg", NT * NG), ("le", NT * NE), ("rev", NE), ("mx", NT),
                        ("eq", NT * NE), ("key", NT * NE), ("km", NT), ("gm", NT * NG), ("gneg", NT * NG),
                        ("em", NT * NE), ("m1", NT), ("m2", NT), ("o1", NT * NE), ("o2", NT * NE), ("gs", NT),
                        ("dl", NT * NG), ("ge", NT * NG), ("dm", NT), ("te", NT), ("w1", NT), ("w2", NT),
                        ("as", NT * NE), ("cnt", NE), ("incl", NE), ("st", NE), ("pos", NT * NE),
                        ("pp", NT * NE), ("p1", NT), ("p2", NT), ("mxg", NT)):
            rtl[name] = (used, n)
            used += n
        assert KD * SLOTP + used <= 3 * KD * T
        rt = blk[:, 5, KD * T - used:KD * T]

        def rv(name):
            a, n = rtl[name]
            return rt[:, a:a + n]

        def rt2(name):
            return rv(name).rearrange("p (t n) -> p t n", t=NT)

        block_ = ctx.enter_context(nc.Block())

        @block_.sync
        def _(sp):
            def slab(n):
                w, c0, _ = SLABS[n]
                if n >= PRE:
                    sp.wait_ge(sem["unit_done"], U[SLABS[n - PRE][2]] + 1)
                sp.dma_start(ring[:, n % PRE, :].rearrange("p (k n) -> p k n", k=KD),
                             w[0].rearrange("(k p) n -> p k n", p=P)[:, :, c0:c0 + 512]
                             ).then_inc(filled[n % PRE], 16)

            def part(e, j, s):
                if j < 2:
                    src = w_gate_up[0, bass.ds(e, 1)].rearrange("a (k p) n -> p (a k) n", p=P)[:, 4 * j:4 * j + 4, :]
                else:
                    src = w_down[0, bass.ds(e, 1)].rearrange("a (k p) n -> p (a k) n", p=P)
                sp.dma_start(slot(s).rearrange("p (k n) -> p k n", k=4), src).then_inc(filled[s], 16)

            for t in range(NT):
                sp.dma_start(xN[:, t, :], x[0, t * P:(t + 1) * P, :]).then_inc(sem["x_loaded"], 16)
            slab(0)
            for tile, row, ap, n in rows:
                sp.dma_start(prow[row:row + n, tile, :], ap).then_inc(sem["par_loaded"], 16)
            early = SLAB_OF["wo1"]
            for n in range(1, early):
                slab(n)
            sp.wait_ge(sem["unit_done"], U["pC0"] + 1)
            for k in (3, 4, 5, 7):
                part(k // PARTS, k % PARTS, k)
            for n in range(early, NSLAB):
                slab(n)
            for k in range(3):
                sp.wait_ge(sem["unit_done"], U[SLABS[NSLAB - PRE + k][2]] + 1)
                part(0, k, k)
            sp.wait_ge(sem["unit_done"], U["rt0"] + 1)
            part(6 // PARTS, 6 % PARTS, 6)

            def refill(k, e):
                used, j = (k - RING) // PARTS, (k - RING) % PARTS
                sp.wait_ge(sem[USED[j]], e + (used + 1))
                part(e + k // PARTS, k % PARTS, k % RING)

            for k in range(RING, PARTS * CYCLE):
                refill(k, 0)
            with sp.Fori(1, NE // CYCLE) as i:
                for k in range(PARTS * CYCLE):
                    refill(k, i * CYCLE)
            sp.wait_ge(sem["ov_ready"], 1)
            n_ov = sp.value_load(ov_i[0:1, 0:1], min_val=0, max_val=NOV)
            with sp.If(n_ov > 0):
                with sp.Fori(0, n_ov) as o:
                    e = sp.value_load(ov_i[0:1, bass.ds(o + 1, 1)], min_val=0, max_val=NE - 1)
                    for j in range(PARTS):
                        sp.wait_ge(sem[USED[j]], o + NE)
                        part(e, j, j)
            for i in range(2 * NT):
                t, c = i // 2, slice(i % 2 * 512, (i % 2 + 1) * 512)
                sp.wait_ge(sem["o_final"], i + 1)
                sp.dma_start(out[0, t * P:(t + 1) * P, c], outN[:, t, c]).then_inc(sem["out_stored"], 16)
            sp.wait_ge(sem["out_stored"], 16 * 2 * NT)

        @block_.gpsimd
        def _(pool):
            g = nc.gpsimd
            g.memset(epsc[:], EPS).then_inc(sem["eps"], 1)
            g.memset(ident[:], 0.0)
            g.memset(ones[:], 1.0)
            g.memset(onesm[:], 1.0 / D)
            g.memset(mask[:], 1.0)
            g.memset(strict[:], 1.0)
            g.memset(sguwT, 0.0)
            g.memset(zeros[:], 0.0)
            g.iota(iota_i, pattern=[[1, SLOTP]], base=0, channel_multiplier=0).then_inc(sem["fills"], 1)
            pool.wait_ge(sem["fills"], 1)
            g.affine_select(out=ident[:], in_=ident[:], compare_op=ALU.not_equal, fill=1.0, base=0,
                            pattern=[[-1, P]], channel_multiplier=1)
            for c in (0, 2):
                g.affine_select(out=mask[:, c * P:(c + 1) * P], in_=mask[:, c * P:(c + 1) * P],
                                compare_op=ALU.is_ge, fill=0.0, base=0, pattern=[[1, P]], channel_multiplier=-1)
            g.affine_select(out=strict[:], in_=strict[:], compare_op=ALU.is_ge, fill=0.0, base=-1,
                            pattern=[[1, P]], channel_multiplier=-1)
            g.tensor_copy(iota_f[:], iota_i).then_inc(sem["consts"], 1)
            pool.wait_ge(read["y"], KD)
            pool.wait_ge(read["z"], 4)
            g.tensor_tensor(out=ycT, in0=ycT, in1=zT, op=ALU.mult).then_inc(sem["yz_ready"], 1)
            pool.wait_ge(sem["unit_done"], U["o3"] + 1)
            g.memset(slotsT[:, :, SLOTS:SLOTP], 0.0).then_inc(sem["pad_ready"], 1)

        @block_.scalar
        def _(act):
            a = nc.scalar
            step = [0]

            def link(ins):
                step[0] += 1
                ins.then_inc(sem["act_step"], 1)
                act.wait_ge(sem["act_step"], step[0])

            def take(name):
                act.wait_ge(sem["unit_done"], U[name] + 1)
                return bank(name)

            def halves(ps):
                return ps[:, :].rearrange("p (f t) -> p f t", f=2)

            def warm(func, c):
                a.activation(stat[:, c:c + 1], epsc[:], func)

            act.wait_ge(sem["eps"], 1)
            warm(ACT.Sqrt, 28)
            act.wait_ge(sem["x_loaded"], 16 * NT)
            for t in range(NT):
                last = a.activation(junk[:, t, :], xN[:, t, :], ACT.Square, accum_out=stat[:, t:t + 1])
            link(last)
            a.activation(stat[:, 2:4], stat[:, 0:2], ACT.Sqrt, bias=epsc[:], scale=1.0 / D).then_inc(sem["x_rms"], 1)
            for dst, ap in small[:SOON]:
                act.dma_start(dst, ap).then_inc(sem["small_loaded"], 16)
            for i in range(2):
                ps = take(f"par{i}")
                n = min(P, npar - i * P)
                a.copy(par[:, i, 0:n], ps[:, 0:n]).then_inc(read["par"], 1)
            act.wait_ge(read["par"], 2)
            for i in range(2):
                ps = take(f"ha{i}")
                for f in range(2):
                    last = a.activation(hT[:, 4 * i + f, :], ps[:, f * T:(f + 1) * T], ACT.Copy,
                                        scale=col("gmix", 4 * i + f))
                last.then_inc(read["ha"], 1)
            for dst, ap in small[SOON:]:
                act.dma_start(dst, ap).then_inc(sem["late_loaded"], 16)

            def conv_init(unit, w, b, f0, acc):
                ps = take(unit)
                for f in range(2):
                    last = a.activation(acc(f0 + f), ps[:, f * T:(f + 1) * T], ACT.Identity,
                                        bias=b(f0 + f), scale=w(f0 + f))
                last.then_inc(sem["conv_init"], 1)

            def silu_xbc(i):
                act.wait_ge(read["xbc"], i + 1)
                for f in range(2 * i, 2 * i + 2):
                    last = a.activation(xbcT(f), xbcT(f), ACT.Silu)
                last.then_inc(sem["silu_ready"], 1)

            link(a.activation(c8[:, 0, :], cols("lam", KD), ACT.Abs))
            link(a.activation(c8[:, 1, :], c8[:, 0, :], ACT.Exp, scale=-1.0))
            a.activation(c8[:, 2, :], c8[:, 1, :], ACT.Ln, bias=1.0).then_inc(sem["lam_ln"], 1)
            act.wait_ge(sem["small_loaded"], 16 * SOON)
            a.activation(dtw[:, 5, 0:HEADS], alog[:], ACT.Exp).then_inc(sem["alog_exp"], 1)
            NX = XBC_TILES // 2
            for i in range(NX):
                conv_init(f"xbc{i}", lambda f: col("ccw", 3 * XBC_TILES + f), lambda f: col("ccb", f), 2 * i, xbcT)
                if i == 2:
                    act.wait_ge(sem["dt_ready"], 1)
                    link(a.activation(dtw[:, 1, :], dtw[:, 0, :], ACT.Abs))
                    link(a.activation(dtw[:, 2, :], dtw[:, 1, :], ACT.Exp, scale=-1.0))
                    a.activation(dtw[:, 3, :], dtw[:, 2, :], ACT.Ln, bias=1.0).then_inc(sem["dt_act"], 1)
                if i >= 2:
                    silu_xbc(i - 2)
            for i in range(KD // 2):
                conv_init(f"xa{i}", lambda f: col("caw", 3 * KD + f), lambda f: col("cab", f), 2 * i,
                          lambda f: xaT[:, f, :])
                if i < 2:
                    silu_xbc(NX - 2 + i)

            def evac(name, dst, func, scale=1.0):
                ps = take(name)
                i = 2 * member(name)
                a.activation(dst[:, i:i + 2, :], halves(ps), func, scale=scale).then_inc(read[family(name)], 1)

            for i in range(2):
                evac(f"z{i}", zT, ACT.Silu)
            for i in range(4):
                ps = take(f"xs{i}")
                a.copy(xsN[:, i // 2, i % 2 * 512:(i % 2 + 1) * 512], ps[:, :]).then_inc(read["xs"], 1)
            for i in range(2, 4):
                evac(f"z{i}", zT, ACT.Silu)
            for i in range(4):
                ps = take(f"v{i}")
                a.activation(vN[:, i % 2, i // 2 * 512:(i // 2 + 1) * 512], ps[:, :],
                             ACT.Gelu_apprx_tanh).then_inc(read["v"], 1)
                for j in (2 * i, 2 * i + 1):
                    ps = take(f"lg{j}")
                    a.activation(gxT[:, j, :], ps[:, 0:T], ACT.Sigmoid, bias=col("gxb", j))
                    a.activation(aT[:, j, :], ps[:, T:2 * T], ACT.Sigmoid, bias=col("gab", j)).then_inc(read["lg"], 1)
            ps = take("wst0")
            wT = ps[:, :].rearrange("p (g t) -> p g t", g=SGU_G)
            a.copy(sguwT[0:CHUNK, :, :], wT[0:CHUNK])
            a.copy(sguwT[CHUNK:P, :, CHUNK:P], wT[CHUNK:P, :, CHUNK:P]).then_inc(read["wst"], 1)
            act.wait_ge(sem["c_ready"], 1)
            act.wait_ge(read["lg"], KD)
            for j in range(KD):
                last = a.activation(a2T[:, j, :], aT[:, j, :], ACT.Exp, scale=c8[:, 5, j:j + 1])
            last.then_inc(sem["a2_ready"], 1)
            act.wait_ge(sem["a2_ready"], 1)
            for j in range(KD):
                last = a.activation(aT[:, j, :], aT[:, j, :], ACT.Exp, scale=c8[:, 4, j:j + 1])
            last.then_inc(sem["a_ready"], 1)

            def exps(i):
                act.wait_ge(read["r"], i + 1)
                v = dec[:, i % 2].rearrange("p h c -> p (h c)")
                a.activation(v, v, ACT.Exp).then_inc(sem["exp_ready"], 1)

            exps(0)
            exps(1)
            evac("u0", uT, ACT.Gelu_apprx_tanh)
            act.wait_ge(sem["a2_min"], 1)
            a.activation(a2T, a2T, ACT.Sqrt, bias=1.0, scale=-1.0).then_inc(sem["mult_ready"], 1)
            act.wait_ge(sem["ln_var"], 1)
            a.activation(stat[:, 8:10], bnag[:, :, 1], ACT.Sqrt, bias=epsc[:]).then_inc(sem["ln_rms"], 1)
            for i in range(1, 4):
                evac(f"u{i}", uT, ACT.Gelu_apprx_tanh)
                exps(i + 1)
            for i in range(4):
                evac(f"ya{i}", yaT, ACT.Gelu_apprx_tanh)
                if i < 3:
                    exps(5 + i)

            def gates(b, h):
                for i in (2 * h, 2 * h + 1):
                    if b == 1:
                        act.wait_ge(read["pA"], i + 1)
                    if b == 2:
                        act.wait_ge(sem["merged_B"], i + 1)
                    evac(f"g{'ABC'[b]}{i}", gateT, ACT.Sigmoid)

            gates(0, 0)
            act.wait_ge(sem["yz_ready"], 1)
            act.wait_ge(sem["yA_ready"], 1)
            a.activation(csq, ycT, ACT.Square).then_inc(sem["csq_ready"], 1)
            gates(0, 1)
            for i in range(2):
                ps = take(f"cn{i}")
                a.activation(crms[:, 2 * i:2 * i + 2, :], halves(ps), ACT.Sqrt, bias=epsc[:],
                             scale=float(GROUPS)).then_inc(read["cn"], 1)
            act.wait_ge(sem["unit_done"], U["pA3"] + 1)
            act.dma_start(memN, mem[0].rearrange("(t p) f -> p t f", p=P)).then_inc(sem["mem_loaded"], 16)
            gates(1, 0)
            act.wait_ge(sem["mem_loaded"], 16)
            for t in range(NT):
                last = a.activation(memnN[:, t, :], memN[:, t, :], ACT.Square, accum_out=stat[:, 10 + t:11 + t])
            link(last)
            a.activation(stat[:, 12:14], stat[:, 10:12], ACT.Sqrt, bias=epsc[:], scale=1.0 / D
                         ).then_inc(sem["mem_rms"], 1)
            gates(1, 1)
            gates(2, 0)
            gates(2, 1)
            act.wait_ge(sem["unit_done"], U["pC3"] + 1)
            for i in range(4):
                act.wait_ge(read["wo"], i + 1)
                a.activation(x1sq[:, 2 * i:2 * i + 2, :], xT[:, 2 * i:2 * i + 2, :], ACT.Square
                             ).then_inc(sem["x1sq_ready"], 1)
            for i in range(2):
                evac(f"k{i}", KT, ACT.Copy)
            ps = take("xn0")
            a.activation(x1rms, ps[:, 0:T], ACT.Sqrt, bias=epsc[:]).then_inc(read["xn"], 1)
            for i in range(2, 4):
                evac(f"k{i}", KT, ACT.Copy)
            for i in range(4):
                evac(f"q{i}", QT, ACT.Copy, scale=float(XA_DH) ** -0.5)
            for h in range(XA_HEADS):
                ps = take(f"sc{h}")
                act.wait_ge(sem["smax_ready"], h + 1)
                for t in range(NT):
                    c = NT * h + t
                    last = a.activation(probs[:, h, t, :], ps[:, t * T:(t + 1) * T], ACT.Exp,
                                        bias=sm[:, 1, c:c + 1], accum_out=sm[:, 2, c:c + 1])
                last.then_inc(read["sc"], 1)
            for i in range(4):
                ps = take(f"va{i}")
                a.copy(VN[:, i % 2, i // 2 * 512:(i // 2 + 1) * 512], ps[:, :]).then_inc(read["va"], 1)
            for h in range(XA_HEADS):
                ps = take(f"pt{h}")
                a.copy(probsT[:, h, :, :], halves(ps)).then_inc(read["pt"], 1)
            warm(ACT.Sqrt, 29)
            for i in range(4):
                act.wait_ge(read["ao"], i + 1)
                a.activation(x2sq[:, 2 * i:2 * i + 2, :], xT[:, 2 * i:2 * i + 2, :], ACT.Square
                             ).then_inc(sem["x2sq_ready"], 1)
            ps = take("rt0")
            a.activation(stat[:, 18:20], ps[:, 128:128 + NT], ACT.Sqrt, bias=epsc[:], scale=1.0 / D
                         ).then_inc(sem["x2_rms"], 1)
            for i in range(4):
                ps = take(f"tr{i}")
                a.copy(x2N[:, i % 2, i // 2 * 512:(i // 2 + 1) * 512], ps[:, :]).then_inc(read["tr"], 1)
            act.wait_ge(sem["gexp_in"], 1)
            a.activation(rv("ge"), rv("dl"), ACT.Exp).then_inc(sem["gexp_done"], 1)
            act.wait_ge(sem["texp_in"], 1)
            a.activation(rv("te"), rv("dm"), ACT.Exp).then_inc(sem["texp_done"], 1)
            act.wait_ge(sem["x2_rinv"], 1)
            act.wait_ge(read["tr"], 4)
            for t in range(NT):
                last = a.activation(h3N[:, t, :], x2N[:, t, :], ACT.Copy, scale=stat[:, 20 + t:21 + t])
            last.then_inc(sem["h3_ready"], 1)
            act.dma_start(gfin, norm_final.partition_broadcast(P)).then_inc(sem["gfin_loaded"], 16)
            for k in range(KD):
                ps = take(f"ga{k}")
                a.activation(slotsT[:, k, 0:SLOTS], ps[:, :], ACT.Copy, scale=col("gffn", k)).then_inc(read["ga"], 1)

            def window_act(n, p):
                act.wait_ge(sem["gu_done"], n + 1)
                a.activation(sil[:, p], gu_bank(p)[:, 0:SEG], ACT.Silu).then_inc(sem["esilu_ready"], 1)
                a.copy(scat[:, p], turn_bank[:, T:2 * T]).then_inc(sem["scat_ready"], 1)
                act.wait_ge(sem["turn_done"], n + 1)
                a.copy(hmT[:, p], turn_bank[:, 0:2 * P].rearrange("p (j c) -> p j c", c=P)
                       ).then_inc(sem["hT_ready"], 1)
                act.wait_ge(sem["dn_done"], n + 1)
                a.copy(yS, down_bank[:, :]).then_inc(sem["yS_ready"], 1)

            a.activation(scat[:, 1], ones[:, 0:1].to_broadcast([P, T]), ACT.Copy, scale=0.0)
            a.activation(yS, ones[:, 0:1].to_broadcast([P, 512]), ACT.Copy, scale=0.0).then_inc(sem["yS_ready"], 1)
            with act.Fori(0, NE // 2) as i:
                for p in range(2):
                    window_act(i * 2 + p, p)
            act.wait_ge(sem["ov_ready"], 1)
            n_ov = act.value_load(ov_i[0:1, 0:1], min_val=0, max_val=NOV)
            with act.If(n_ov > 0):
                with act.Fori(0, n_ov) as o:
                    window_act(o + NE, 0)
            warm(ACT.Sqrt, 31)
            for i in range(2 * NT):
                t, h = i // 2, i % 2
                act.wait_ge(sem["x3_done"], i + 1)
                last = a.activation(junk3[:, t, h * 512:(h + 1) * 512], x3_bank[i][:, :], ACT.Square,
                                    accum_out=sq3[:, i:i + 1])
                if h:
                    last.then_inc(sem["x3sq_ready"], 1)
                    act.wait_ge(sem["x3sum_ready"], t + 1)
                    a.activation(stat[:, 24 + t:25 + t], stat[:, 22 + t:23 + t], ACT.Sqrt, bias=epsc[:],
                                 scale=1.0 / D).then_inc(sem["x3_rms"], 1)

        @block_.vector
        def _(dve):
            v = nc.vector
            step = [0]

            def link(ins):
                step[0] += 1
                ins.then_inc(sem["dve_step"], 1)
                dve.wait_ge(sem["dve_step"], step[0])

            def take(name):
                dve.wait_ge(sem["unit_done"], U[name] + 1)
                return bank(name)

            def halves(ps):
                return ps[:, :].rearrange("p (f t) -> p f t", f=2)

            dve.wait_ge(sem["x_rms"], 1)
            link(v.reciprocal(stat[:, 4:6], stat[:, 2:4]))
            for t in range(NT):
                v.tensor_scalar(xnN[:, t, :], xN[:, t, :], stat[:, 4 + t:5 + t], None, ALU.mult
                                ).then_inc(sem["xn_ready"], 1)
            dve.wait_ge(read["par"], 2)
            for i in range(2):
                ps = take(f"hb{i}")
                for f in range(2):
                    last = v.tensor_scalar(hT[:, 4 * i + 2 + f, :], ps[:, f * T:(f + 1) * T],
                                           col("gmix", 4 * i + 2 + f), None, ALU.mult)
                last.then_inc(read["hb"], 1)
            link(v.tensor_scalar(c8[:, 3, :], cols("lam", KD), -1.0, 0.0, ALU.mult, ALU.max))
            dve.wait_ge(sem["lam_ln"], 1)
            link(v.tensor_tensor(c8[:, 3, :], c8[:, 3, :], c8[:, 2, :], ALU.add))
            v.tensor_scalar(c8[:, 4, :], c8[:, 3, :], -LRU_C, None, ALU.mult)
            v.tensor_scalar(c8[:, 5, :], c8[:, 3, :], -2 * LRU_C, None, ALU.mult).then_inc(sem["c_ready"], 1)
            dve.wait_ge(sem["small_loaded"], 16 * SOON)
            pairs = dsk[:, :].rearrange("p (f h) -> p f h", h=P // HD)
            for h in range(P // HD):
                last = v.tensor_copy(dcol[h * HD:(h + 1) * HD, :], pairs[h * HD:(h + 1) * HD, :, h])
            last.then_inc(sem["d_ready"], 1)

            convs = [0]

            def taps(unit, w, tiles_, f0, acc):
                convs[0] += 1
                dve.wait_ge(sem["conv_init"], convs[0])
                ps = bank(unit)
                for j in range(1, CONV):
                    for f in range(2):
                        last = v.scalar_tensor_tensor(
                            out=acc(f0 + f)[:, j:], in0=ps[:, f * T:(f + 1) * T - j],
                            scalar=col(w, (CONV - 1 - j) * tiles_ + f0 + f), in1=acc(f0 + f)[:, j:],
                            op0=ALU.mult, op1=ALU.add)
                    if j < CONV - 1:
                        link(last)
                last.then_inc(read[family(unit)], 1)

            NX = XBC_TILES // 2
            for i in range(NX):
                taps(f"xbc{i}", "ccw", XBC_TILES, 2 * i, xbcT)
                if i == 1:
                    ps = take("dt0")
                    last = (v.tensor_tensor(dtw[:, 0, :].rearrange("p (t h) -> p t h", t=NT),
                                         ps[:, 0:NT * HEADS].rearrange("p (t h) -> p t h", t=NT),
                                         dtb[:, :].rearrange("p (o h) -> p o h", o=1).to_broadcast([P, NT, HEADS]),
                                         ALU.add))
                    last.then_inc(read["dt"], 1)
                    dve.wait_ge(read["dt"], 1)
                    v.tensor_scalar(dtw[:, 4, :], dtw[:, 0, :], 0.0, None, ALU.max).then_inc(sem["dt_ready"], 1)
                if i == 4:
                    dve.wait_ge(sem["dt_act"], 1)
                    link(v.tensor_tensor(dtw[:, 4, :], dtw[:, 4, :], dtw[:, 3, :], ALU.add))
                    dve.wait_ge(sem["alog_exp"], 1)
                    for t in range(NT):
                        c = slice(t * HEADS, (t + 1) * HEADS)
                        last = v.scalar_tensor_tensor(out=dtw[:, 6, c], in0=dtw[:, 4, c], scalar=-1.0,
                                                      in1=dtw[:, 5, 0:HEADS], op0=ALU.mult, op1=ALU.mult)
                    last.then_inc(sem["dta_ready"], 1)
            dve.wait_ge(sem["late_loaded"], 16 * (len(small) - SOON))
            for k in range(KD):
                last = v.tensor_scalar(wr[:, k, :], wr[:, k, :], col("gffn", k), None, ALU.mult)
            last.then_inc(sem["wr_ready"], 1)
            for i in range(KD // 2):
                taps(f"xa{i}", "caw", KD, 2 * i, lambda f: xaT[:, f, :])
            ps = take("cs0")
            v.tensor_copy(csN[:, :, :], ps[:, 0:NT * HEADS].rearrange("p (t h) -> p t h", t=NT)
                          ).then_inc(read["cs"], 1)
            for i in range(4):
                ps = take(f"xt{i}")
                v.tensor_copy(xT[:, 2 * i:2 * i + 2, :], halves(ps)).then_inc(read["xt"], 1)
            for g in range(GROUPS):
                ps = take(f"cb{g}")
                v.tensor_tensor(cbm[:, g, :], ps[:, 0:3 * P], mask[:, :], ALU.mult).then_inc(read["cb"], 1)

            dve.wait_ge(read["lg"], KD)
            link(v.tensor_tensor(gxT, gxT, xaT, ALU.mult))
            def exponents(i):
                ps = take(f"r{i}")
                if i >= 2:
                    dve.wait_ge(sem["unit_done"], U[f"y{i - 2}"] + 1)
                for h in range(2):
                    c = csN[:, :, 2 * i + h:2 * i + h + 1]
                    v.tensor_scalar(dec[:, i % 2, h, 0:T], ps[:, h * T:(h + 1) * T], c[:, 0, :], 0.0,
                                    ALU.subtract, ALU.min)
                    last = v.tensor_scalar(dec[:, i % 2, h, T:], ps[:, h * T + P:(h + 1) * T], c[:, 1, :], 0.0,
                                           ALU.subtract, ALU.min)
                last.then_inc(read["r"], 1)

            def weights(i):
                dve.wait_ge(sem["exp_ready"], i + 1)
                for h in range(2):
                    hd = 2 * i + h
                    for t, c in ((0, slice(0, T)), (1, slice(T, 3 * P))):
                        last = v.scalar_tensor_tensor(
                            out=dec[:, i % 2, h, c], in0=dec[:, i % 2, h, c],
                            scalar=dtw[:, 4, t * HEADS + hd:t * HEADS + hd + 1], in1=cbm[:, hd // HPG, c],
                            op0=ALU.mult, op1=ALU.mult)
                last.then_inc(sem["w_ready"], 1)

            def skip(i):
                ps = take(f"y{i}")
                v.scalar_tensor_tensor(out=ycT[:, i, :], in0=xbcT(i), scalar=dcol[:, i:i + 1], in1=ps[:, 0:T],
                                       op0=ALU.mult, op1=ALU.add).then_inc(read["y"], 1)

            dve.wait_ge(read["cs"], 1)
            dve.wait_ge(read["cb"], GROUPS)
            exponents(0)
            exponents(1)
            weights(0)
            skip(0)
            exponents(2)
            dve.wait_ge(sem["a2_ready"], 1)
            v.tensor_scalar(a2T, a2T, 1.0, None, ALU.min).then_inc(sem["a2_min"], 1)
            dve.wait_ge(read["v"], 4)
            for t in range(NT):
                for h in range(2):
                    last = v.bn_stats(bnst[:, t, h, :], vN[:, t, h * 512:(h + 1) * 512])
            link(last)
            for t in range(NT):
                last = v.bn_aggr(bnag[:, t, :], bnst[:, t, :, :])
            last.then_inc(sem["ln_var"], 1)
            weights(1)
            skip(1)
            exponents(3)
            dve.wait_ge(sem["ln_rms"], 1)
            link(v.reciprocal(stat[:, 6:8], stat[:, 8:10]))
            for t in range(NT):
                last = v.tensor_scalar(vN[:, t, :], vN[:, t, :], bnag[:, t, 0:1], stat[:, 6 + t:7 + t],
                                       ALU.subtract, ALU.mult)
            last.then_inc(sem["vn_ready"], 1)
            dve.wait_ge(sem["mult_ready"], 1)
            link(v.tensor_tensor(gxT, gxT, a2T, ALU.mult))
            dve.wait_ge(sem["a_ready"], 1)
            scans = list(range(KD))

            def scan(n):
                for j in scans[:n]:
                    v.tensor_tensor_scan(xaT[:, j, :], aT[:, j, :], gxT[:, j, :], 0.0, ALU.mult, ALU.add)
                del scans[:n]

            for i in range(2, KD):
                weights(i)
                scan(1)
                skip(i)
                if i + 2 < KD:
                    exponents(i + 2)
            dve.wait_ge(read["u"], 4)
            for g in range(SGU_G):
                ps = take(f"sg{g}")
                bias = sgub[:, g:g + 1, :].to_broadcast([P, NT, SGU_BLOCK])
                for f in range(2):
                    half = ps[:, f * T:(f + 1) * T].rearrange("p (n t) -> p n t", n=NT)
                    last = v.scalar_tensor_tensor(out=half, in0=half, scalar=col("gsgu", 2 * g + f), in1=bias,
                                                  op0=ALU.mult, op1=ALU.add)
                link(last)
                v.tensor_tensor(uT[:, 2 * g:2 * g + 2, :], uT[:, 2 * g:2 * g + 2, :], halves(ps), ALU.mult
                                ).then_inc(read["sg"], 1)
            v.tensor_tensor_scan(xaT[:, scans[0], :], aT[:, scans[0], :], gxT[:, scans[0], :], 0.0,
                                 ALU.mult, ALU.add)
            link(v.tensor_tensor_scan(xaT[:, scans[1], :], aT[:, scans[1], :], gxT[:, scans[1], :], 0.0,
                                      ALU.mult, ALU.add))
            dve.wait_ge(read["ya"], 4)
            v.tensor_tensor(xaT, xaT, yaT, ALU.mult).then_inc(sem["yA_ready"], 1)

            def merge(b, h):
                for i in (2 * h, 2 * h + 1):
                    s = slice(2 * i, 2 * i + 2)
                    n = "ABC"[b]
                    ps = take(f"p{n}{i}")
                    dve.wait_ge(read["g" + n], i + 1)
                    if b == 0:
                        v.tensor_tensor(mergedT[:, s, :], gateT[:, s, :], halves(ps), ALU.mult
                                        ).then_inc(read["pA"], 1)
                        continue
                    v.tensor_tensor(gateT[:, s, :], gateT[:, s, :], halves(ps), ALU.mult).then_inc(read["p" + n], 1)
                    dve.wait_ge(read["p" + n], i + 1)
                    v.tensor_tensor(mergedT[:, s, :], mergedT[:, s, :], gateT[:, s, :], ALU.add
                                    ).then_inc(sem["merged_" + n], 1)

            merge(0, 0)
            merge(0, 1)
            dve.wait_ge(read["cn"], 2)
            link(v.reciprocal(crms, crms))
            for f in range(KD):
                last = v.scalar_tensor_tensor(out=ycT[:, f, :], in0=ycT[:, f, :], scalar=col("gssm", f),
                                              in1=crms[:, f * GROUPS // KD, :], op0=ALU.mult, op1=ALU.mult)
            last.then_inc(sem["yC_ready"], 1)
            merge(1, 0)
            dve.wait_ge(sem["mem_rms"], 1)
            link(v.reciprocal(stat[:, 14:16], stat[:, 12:14]))
            for t in range(NT):
                v.tensor_scalar(memnN[:, t, :], memN[:, t, :], stat[:, 14 + t:15 + t], None, ALU.mult
                                ).then_inc(sem["memn_ready"], 1)
            merge(1, 1)
            for i in range(4):
                ps = take(f"mt{i}")
                for f in range(2):
                    last = v.tensor_scalar(memT[:, 2 * i + f, :], ps[:, f * T:(f + 1) * T], col("gmem", 2 * i + f),
                                           None, ALU.mult)
                last.then_inc(read["mt"], 1)
            merge(2, 0)
            merge(2, 1)

            def add_x(name):
                ps = take(name)
                s = slice(2 * member(name), 2 * member(name) + 2)
                v.tensor_tensor(xT[:, s, :], xT[:, s, :], halves(ps), ALU.add).then_inc(read[family(name)], 1)

            for i in range(4):
                add_x(f"wo{i}")
            dve.wait_ge(read["xn"], 1)
            link(v.reciprocal(x1rms, x1rms))
            for f in range(KD):
                v.scalar_tensor_tensor(out=hxT[:, f, :], in0=xT[:, f, :], scalar=col("gxa", f), in1=x1rms,
                                       op0=ALU.mult, op1=ALU.mult).then_inc(sem["hx_ready"], 1)
            for h in range(XA_HEADS + 1):
                if h < XA_HEADS:
                    ps = take(f"sc{h}")
                    c = slice(NT * h, NT * h + NT)
                    link(v.reduce_max(sm[:, 0, c], ps[:, :].rearrange("p (t m) -> p t m", t=NT), AX.X))
                    v.tensor_scalar(sm[:, 1, c], sm[:, 0, c], -1.0, None, ALU.mult).then_inc(sem["smax_ready"], 1)
                if h > 0:
                    c = slice(NT * (h - 1), NT * h)
                    dve.wait_ge(read["sc"], h)
                    link(v.reciprocal(sm[:, 3, c], sm[:, 2, c]))
                    for t in range(NT):
                        last = v.tensor_scalar(probs[:, h - 1, t, :], probs[:, h - 1, t, :],
                                               sm[:, 3, NT * (h - 1) + t:NT * (h - 1) + t + 1], None, ALU.mult)
                    last.then_inc(sem["p_ready"], 1)
            for h in range(XA_HEADS):
                ps = take(f"o{h}")
                v.tensor_copy(oT[:, 2 * h:2 * h + 2, :], halves(ps)).then_inc(read["o"], 1)
            for i in range(4):
                add_x(f"ao{i}")
            dve.wait_ge(sem["x2_rms"], 1)
            v.reciprocal(stat[:, 20:22], stat[:, 18:20]).then_inc(sem["x2_rinv"], 1)
            dve.wait_ge(sem["x2_rinv"], 1)
            ps = take("rt0")
            lf = rt2("l")
            for t in range(NT):
                last = v.scalar_tensor_tensor(out=lf[:, t, :], in0=ps[:, t * 64:t * 64 + NG + NE],
                                              scalar=stat[:, 20 + t:21 + t], in1=br[:, :], op0=ALU.mult, op1=ALU.add)
            last.then_inc(read["rt"], 1)
            dve.wait_ge(read["rt"], 1)
            gl = rt2("lg")
            v.tensor_copy(gl, lf[:, :, 0:NG])
            v.tensor_copy(rt2("le"), lf[:, :, NG:])
            link(v.tensor_scalar(rv("rev"), iota_f[:, 0:NE], -1.0, float(NE), ALU.mult, ALU.add))

            def wide(name, n):
                return rv(name).rearrange("p (t o) -> p t o", o=1).to_broadcast([P, NT, n])

            def first_hot(src, n, mx, hot):
                link(v.reduce_max(rv(mx), src, AX.X))
                eq = rv("eq")[:, 0:NT * n].rearrange("p (t n) -> p t n", t=NT)
                key = rv("key")[:, 0:NT * n].rearrange("p (t n) -> p t n", t=NT)
                link(v.tensor_tensor(eq, src, wide(mx, n), ALU.is_equal))
                rev = rv("rev")[:, 0:n].rearrange("p (o n) -> p o n", o=1).to_broadcast([P, NT, n])
                link(v.tensor_tensor(key, eq, rev, ALU.mult))
                link(v.reduce_max(rv("km"), key, AX.X))
                link(v.tensor_tensor(hot, key, wide("km", n), ALU.is_equal))

            first_hot(gl, NG, "mxg", rt2("gm"))
            v.tensor_tensor(rt2("dl"), gl, wide("mxg", NG), ALU.subtract).then_inc(sem["gexp_in"], 1)
            link(v.tensor_scalar(rv("gneg"), rv("gm"), BIG, -BIG, ALU.mult, ALU.add))
            em3 = rv("em").rearrange("p (g e) -> p g e", e=EPG)

            def over(name):
                return rv(name).rearrange("p (g o) -> p g o", o=1).to_broadcast([P, NT * NG, EPG])

            link(v.tensor_tensor(em3, rv("le").rearrange("p (g e) -> p g e", e=EPG), over("gm"), ALU.mult))
            link(v.tensor_tensor(em3, em3, over("gneg"), ALU.add))
            first_hot(rt2("em"), NE, "m1", rt2("o1"))
            link(v.scalar_tensor_tensor(out=rv("em"), in0=rv("o1"), scalar=-3 * BIG, in1=rv("em"),
                                        op0=ALU.mult, op1=ALU.add))
            first_hot(rt2("em"), NE, "m2", rt2("o2"))
            v.tensor_tensor(rv("as"), rv("o1"), rv("o2"), ALU.add).then_inc(sem["assign_ready"], 1)
            v.tensor_tensor(rv("dm"), rv("m2"), rv("m1"), ALU.subtract).then_inc(sem["texp_in"], 1)
            dve.wait_ge(sem["gexp_done"], 1)
            link(v.reduce_sum(rv("gs"), rt2("ge"), AX.X))
            link(v.reciprocal(rv("gs"), rv("gs")))
            dve.wait_ge(sem["texp_done"], 1)
            link(v.tensor_scalar(rv("w1"), rv("te"), 1.0, None, ALU.add))
            link(v.reciprocal(rv("w1"), rv("w1")))
            link(v.tensor_tensor(rv("w1"), rv("w1"), rv("gs"), ALU.mult))
            link(v.tensor_tensor(rv("w2"), rv("w1"), rv("te"), ALU.mult))
            ps = take("rk0")
            link(v.tensor_copy(rv("cnt"), ps[:, 2 * NE:3 * NE]))
            link(v.tensor_tensor_scan(rv("incl"), ones[:, 0:NE], rv("cnt"), 0.0, ALU.mult, ALU.add))
            link(v.tensor_tensor(rv("st"), rv("incl"), rv("cnt"), ALU.subtract))
            v.tensor_tensor(rt2("pos"), ps[:, 0:2 * NE].rearrange("p (t n) -> p t n", t=NT),
                            rv("st").rearrange("p (o n) -> p o n", o=1).to_broadcast([P, NT, NE]), ALU.add
                            ).then_inc(read["rk"], 1)
            dve.wait_ge(read["rk"], 1)
            for hot, p in (("o1", "p1"), ("o2", "p2")):
                link(v.tensor_tensor(rv("pp"), rv(hot), rv("pos"), ALU.mult))
                link(v.reduce_sum(rv(p), rt2("pp"), AX.X))
            for t in range(NT):
                last = v.tensor_scalar(sel[:, t, :], iota_f[:, 0:SLOTS], rv("p1")[:, t:t + 1], None, ALU.is_equal)
            link(last)
            for t in range(NT):
                v.scalar_tensor_tensor(out=sel[:, t, :], in0=iota_f[:, 0:SLOTS], scalar=rv("p2")[:, t:t + 1],
                                       in1=sel[:, t, :], op0=ALU.is_equal, op1=ALU.add).then_inc(sem["sel_ready"], 1)
            v.memset(pw[:, :, NE:NE + 1], 0.0)
            v.tensor_copy(pw[:, 0:NT, 0:NE], rt2("pos"))
            for t in range(NT):
                link(v.tensor_scalar(rt2("pp")[:, t, :], rt2("o1")[:, t, :], rv("w1")[:, t:t + 1], None, ALU.mult))
                link(v.scalar_tensor_tensor(out=pw[:, NT + t, 0:NE], in0=rt2("o2")[:, t, :],
                                            scalar=rv("w2")[:, t:t + 1], in1=rt2("pp")[:, t, :],
                                            op0=ALU.mult, op1=ALU.add))
            v.tensor_copy(starts_i[0:1, 0:NE], rv("st")[0:1, :])
            link(v.memset(starts_i[0:1, NE:NE + 1], 0))

            def ov(i, n=1):
                return ovf[0:1, i * NCAND:(i + n) * NCAND]

            st1, cnt1 = rv("st")[0:1, :], rv("cnt")[0:1, :]
            for j in range(1, T // WIN):
                c = slice((j - 1) * NE, j * NE)
                v.tensor_scalar(ov(0)[:, c], cnt1, float(WIN * j), None, ALU.is_gt)
                v.tensor_scalar(ov(1)[:, c], st1, float(WIN * j), None, ALU.add)
                last = v.tensor_copy(ov(3)[:, c], iota_f[0:1, 0:NE])
            link(last)
            link(v.memset(ov(5), 1.0))
            link(v.tensor_tensor_scan(ov(4), ov(5), ov(0), 0.0, ALU.mult, ALU.add))
            link(v.tensor_tensor(ov(6), ov(4), ov(0), ALU.mult))
            big = ovf[0:1, 8 * NCAND:(8 + NOV) * NCAND].rearrange("p (o c) -> p o c", c=NCAND)
            big2 = ovf2.rearrange("p (o c) -> p o c", c=NCAND)

            def each(i):
                return ov(i).rearrange("p (o c) -> p o c", o=1).to_broadcast([1, NOV, NCAND])

            place = iota_f[0:1, 1:NOV + 1].rearrange("p (o c) -> p o c", c=1).to_broadcast([1, NOV, NCAND])
            link(v.tensor_tensor(big, each(6), place, ALU.is_equal))
            link(v.tensor_tensor(big2, big, each(3), ALU.mult))
            link(v.reduce_sum(ov(7)[:, 1:NOV + 1], big2, AX.X))
            link(v.tensor_tensor(big2, big, each(1), ALU.mult))
            link(v.reduce_sum(ov(7)[:, NOV + 1:2 * NOV + 1], big2, AX.X))
            link(v.tensor_copy(ov(7)[:, 0:1], ov(4)[:, NCAND - 1:NCAND]))
            v.tensor_copy(ov_i[0:1, 0:2 * NOV + 1], ov(7)[:, 0:2 * NOV + 1]).then_inc(sem["ov_ready"], 1)

            dve.wait_ge(sem["ov_ready"], 1)
            dve.wait_ge(sem["pad_ready"], 1)

            def window(n, e, start, p):
                v.tensor_copy(chosen[:, p], pw[:, :, bass.ds(e, 1)].rearrange("p a o -> p (a o)")
                              ).then_inc(sem["chosen_ready"], 1)
                v.tensor_copy(xe[:, p], slotsT[:, :, bass.ds(start, WIN)]).then_inc(sem["xe_ready"], 1)
                dve.wait_ge(sem["chosen_ready"], n + 1)
                slots = iota_f[:, bass.ds(start, WIN)].rearrange("p (d w) -> p d w", d=1).to_broadcast([P, 2, WIN])
                for t in range(NT):
                    last = v.tensor_scalar(placed[:, p, t], slots, chosen[:, p, t:t + 1], chosen[:, p, NT + t:NT + t + 1],
                                           ALU.is_equal, ALU.mult)
                last.then_inc(sem["placed_ready"], 1)

            def first_slot(e):
                return dve.value_load(starts_i[0:1, bass.ds(e, 1)], min_val=0, max_val=SLOTS)

            def hidden(n, p):
                dve.wait_ge(sem["esilu_ready"], n + 1)
                v.tensor_tensor(hm[:, p], sil[:, p], gu_bank(p)[:, SEG:2 * SEG], ALU.mult).then_inc(sem["h_ready"], 1)

            first = first_slot(0)
            dve.wait_ge(read["ga"], KD)
            window(0, 0, first, 0)
            with dve.Fori(0, NE // 2) as i:
                for p in range(2):
                    e = i * 2 + (p + 1)
                    window(e, e, first_slot(e), 1 - p)
                    hidden(i * 2 + p, p)
            n_ov = dve.value_load(ov_i[0:1, 0:1], min_val=0, max_val=NOV)
            with dve.If(n_ov > 0):
                with dve.Fori(0, n_ov) as o:
                    e = dve.value_load(ov_i[0:1, bass.ds(o + 1, 1)], min_val=0, max_val=NE - 1)
                    s = dve.value_load(ov_i[0:1, bass.ds(o + (NOV + 1), 1)], min_val=0, max_val=SLOTS)
                    window(o + (NE + 1), e, s, 1)
                    hidden(o + NE, 0)
            dve.wait_ge(sem["gfin_loaded"], 16)
            for t in range(NT):
                dve.wait_ge(sem["x3sq_ready"], t + 1)
                v.tensor_tensor(stat[:, 22 + t:23 + t], sq3[:, 2 * t:2 * t + 1], sq3[:, 2 * t + 1:2 * t + 2], ALU.add
                                ).then_inc(sem["x3sum_ready"], 1)
                dve.wait_ge(sem["x3_rms"], t + 1)
                link(v.reciprocal(stat[:, 26 + t:27 + t], stat[:, 24 + t:25 + t]))
                for h in range(2):
                    c = slice(h * 512, (h + 1) * 512)
                    v.scalar_tensor_tensor(out=outN[:, t, c], in0=x3_bank[2 * t + h][:, :], scalar=stat[:, 26 + t:27 + t],
                                           in1=gfin[:, c], op0=ALU.mult, op1=ALU.mult).then_inc(sem["o_final"], 1)

        @block_.tensor
        def _(pe):
            mm, tp = nc.tensor.matmul, nc.tensor.transpose
            count = [0]

            def begin(name):
                assert order[count[0]] == name
                before = [i for i in range(count[0]) if BANK[i] == BANK[count[0]]]
                if before:
                    last = order[before[-1]]
                    pe.wait_ge(read[family(last)], member(last) + 1)
                count[0] += 1
                return bank(name)

            def end(ins):
                ins.then_inc(sem["unit_done"], 1)

            def slab_of(n):
                pe.wait_ge(filled[n % PRE], 16 * (n // PRE + 1))
                return ring[:, n % PRE, :].rearrange("p (k n) -> p k n", k=KD)

            def dense(name, src):
                i = member(name)
                first = name if i % 2 else family(name) + str(i + 1)
                w = slab_of(SLAB_OF[first])
                ps = begin(name)
                for f in range(2):
                    c = (2 * (i % 2) + f) * P
                    for k in range(KD):
                        last = mm(ps[:, f * T:(f + 1) * T], w[:, k, c:c + P], src[:, k, :],
                                  start=k == 0, stop=k == KD - 1)
                end(last)

            def dense_rows(name, src):
                i = member(name)
                first = name if i % 2 else family(name) + str(i + 1)
                w = slab_of(SLAB_OF[first])
                ps = begin(name)
                t = i % 2
                for k in range(KD):
                    last = mm(ps[:, :], src[:, k, t * P:(t + 1) * P], w[:, k, :], start=k == 0, stop=k == KD - 1)
                end(last)

            def to_T(name, src):
                ps = begin(name)
                i = TILEPAIR[name]
                for f in range(2):
                    for t in range(NT):
                        last = tp(ps[:, f * T + t * P:f * T + (t + 1) * P],
                                  src[:, t, (2 * i + f) * P:(2 * i + f + 1) * P], ident[:])
                end(last)

            def to_N(name, t, tile, h):
                ps = begin(name)
                for f in range(4):
                    last = tp(ps[:, f * P:(f + 1) * P], tile(4 * h + f)[:, t * P:(t + 1) * P], ident[:])
                end(last)

            TILEPAIR = {"ha0": 0, "hb0": 1, "ha1": 2, "hb1": 3}
            for i in range(4):
                TILEPAIR[f"xt{i}"] = TILEPAIR[f"mt{i}"] = i

            pe.wait_ge(sem["consts"], 1)
            pe.wait_ge(sem["xn_ready"], NT)
            to_T("ha0", xnN)
            to_T("hb0", xnN)
            pe.wait_ge(sem["par_loaded"], 16 * len(rows))
            for i in range(2):
                ps = begin(f"par{i}")
                n = min(P, npar - i * P)
                end(tp(ps[:, 0:n], prow[0:n, i, :], ident[0:n, 0:n]))
            to_T("ha1", xnN)
            to_T("hb1", xnN)
            pe.wait_ge(read["ha"], 2)
            pe.wait_ge(read["hb"], 2)
            for i in range(8):
                dense(f"xbc{i}", hT)
                if i == 1:
                    pe.wait_ge(sem["small_loaded"], 16 * SOON)
                    ps = begin("dt0")
                    for t in range(NT):
                        for k in range(KD):
                            last = mm(ps[:, t * HEADS:(t + 1) * HEADS], hT[:, k, t * P:(t + 1) * P], wdt[:, k, :],
                                      start=k == 0, stop=k == KD - 1)
                    end(last)
            for i in range(4):
                dense(f"xa{i}", hT)
            pe.wait_ge(sem["dta_ready"], 1)
            dta = dtw[:, 6, :].rearrange("p (t h) -> p t h", t=NT)
            ps = begin("cs0")
            mm(ps[:, 0:HEADS], mask[:, 0:P], dta[:, 0, :], start=True, stop=True)
            mm(ps[:, HEADS:2 * HEADS], ones[:], dta[:, 0, :], start=True, stop=False)
            end(mm(ps[:, HEADS:2 * HEADS], mask[:, 0:P], dta[:, 1, :], start=False, stop=True))
            for i in range(4):
                to_T(f"xt{i}", xN)
            for i in range(2):
                dense(f"z{i}", hT)
            pe.wait_ge(sem["silu_ready"], XBC_TILES // 2)
            for i in range(4):
                to_N(f"xs{i}", i // 2, xbcT, i % 2)
            for i in range(2, 4):
                dense(f"z{i}", hT)
            for g in range(GROUPS):
                ps = begin(f"cb{g}")
                bT, cT = xbcT(KD + g), xbcT(KD + GROUPS + g)
                mm(ps[:, 0:T], bT[:, 0:P], cT, start=True, stop=True)
                end(mm(ps[:, T:3 * P], bT[:, P:T], cT[:, P:T], start=True, stop=True))
            pe.wait_ge(sem["late_loaded"], 16 * (len(small) - SOON))
            pe.wait_ge(read["xa"], 4)
            pe.wait_ge(read["xt"], 4)
            for i in range(4):
                dense_rows(f"v{i}", hT)
                for j in (2 * i, 2 * i + 1):
                    ps = begin(f"lg{j}")
                    mm(ps[:, 0:T], gxw[:, j, :], xaT[:, j, :], start=True, stop=True)
                    end(mm(ps[:, T:2 * T], gaw[:, j, :], xaT[:, j, :], start=True, stop=True))
            ps = begin("wst0")
            for g in range(SGU_G):
                last = tp(ps[:, g * P:(g + 1) * P], sguw[:, g, :], ident[:])
            end(last)

            def cum(i):
                ps = begin(f"r{i}")
                for h in range(2):
                    hd = 2 * i + h
                    mm(ps[:, h * T:(h + 1) * T], dta[:, 0, hd:hd + 1].to_broadcast([P, P]), mask[:, 0:T],
                       start=True, stop=False)
                    last = mm(ps[:, h * T + P:(h + 1) * T], dta[:, 1, hd:hd + 1].to_broadcast([P, P]), mask[:, 0:P],
                              start=False, stop=True)
                end(last)

            def heads(i):
                pe.wait_ge(sem["w_ready"], i + 1)
                ps = begin(f"y{i}")
                for h in range(2):
                    hd = 2 * i + h
                    o = ps[h * HD:(h + 1) * HD, :]
                    mm(o[:, 0:T], xsN[:, 0, hd * HD:(hd + 1) * HD], dec[:, i % 2, h, 0:T], start=True, stop=False)
                    last = mm(o[:, P:T], xsN[:, 1, hd * HD:(hd + 1) * HD], dec[:, i % 2, h, T:], start=False, stop=True)
                end(last)

            pe.wait_ge(read["xs"], 4)
            dense("u0", hT)
            cum(0)
            cum(1)
            for i in range(1, 4):
                dense(f"u{i}", hT)
                heads(i - 1)
                cum(i + 1)
            for i in range(3):
                dense(f"ya{i}", hT)
                heads(3 + i)
                cum(5 + i)
            dense("ya3", hT)
            heads(6)
            pe.wait_ge(sem["vn_ready"], 1)
            pe.wait_ge(read["wst"], 1)
            for g in range(SGU_G):
                ps = begin(f"sg{g}")
                for f in range(2):
                    for n in range(NT):
                        last = mm(ps[:, f * T + n * P:f * T + (n + 1) * P], vN[:, n, (2 * g + f) * P:(2 * g + f + 1) * P],
                                  sguwT[:, g, :], start=True, stop=True)
                end(last)
            heads(7)

            def branch(b, src, ready, n):
                for h in range(2):
                    for i in (2 * h, 2 * h + 1):
                        dense(f"g{b}{i}", hT)
                    pe.wait_ge(ready, n)
                    for i in (2 * h, 2 * h + 1):
                        dense(f"p{b}{i}", src)

            branch("A", xaT, sem["yA_ready"], 1)
            pe.wait_ge(sem["csq_ready"], 1)
            for i in range(2):
                ps = begin(f"cn{i}")
                for g in range(2):
                    for f in range(2):
                        last = mm(ps[:, g * T:(g + 1) * T], onesm[:], csq[:, 4 * i + 2 * g + f, :],
                                  start=f == 0, stop=f == 1)
                end(last)
            branch("B", uT, read["sg"], SGU_G)
            pe.wait_ge(sem["memn_ready"], NT)
            for i in range(4):
                to_T(f"mt{i}", memnN)
            branch("C", ycT, sem["yC_ready"], 1)
            pe.wait_ge(sem["merged_C"], 4)
            for i in range(4):
                dense(f"wo{i}", mergedT)
            pe.wait_ge(read["mt"], 4)
            for i in range(2):
                dense(f"k{i}", memT)
            pe.wait_ge(sem["x1sq_ready"], 4)
            ps = begin("xn0")
            for k in range(KD):
                last = mm(ps[:, 0:T], onesm[:], x1sq[:, k, :], start=k == 0, stop=k == KD - 1)
            end(last)
            for i in range(2, 4):
                dense(f"k{i}", memT)
            pe.wait_ge(sem["hx_ready"], KD)
            for i in range(4):
                dense(f"q{i}", hxT)
            pe.wait_ge(read["q"], 4)
            pe.wait_ge(read["k"], 4)
            for h in range(XA_HEADS):
                ps = begin(f"sc{h}")
                for t in range(NT):
                    for j in range(2):
                        last = mm(ps[:, t * T:(t + 1) * T], QT[:, 2 * h + j, t * P:(t + 1) * P], KT[:, 2 * h + j, :],
                                  start=j == 0, stop=j == 1)
                end(last)
            for i in range(4):
                dense_rows(f"va{i}", memT)

            def turn(h):
                pe.wait_ge(sem["p_ready"], h + 1)
                ps = begin(f"pt{h}")
                for j in range(NT):
                    for t in range(NT):
                        last = tp(ps[:, j * T + t * P:j * T + (t + 1) * P], probs[:, h, t, j * P:(j + 1) * P], ident[:])
                end(last)

            def attend(h):
                pe.wait_ge(read["pt"], h + 1)
                ps = begin(f"o{h}")
                for f in range(2):
                    for j in range(NT):
                        last = mm(ps[:, f * T:(f + 1) * T], VN[:, j, (2 * h + f) * P:(2 * h + f + 1) * P],
                                  probsT[:, h, j, :], start=j == 0, stop=j == NT - 1)
                end(last)

            turn(0)
            pe.wait_ge(read["va"], 4)
            for h in range(1, XA_HEADS):
                turn(h)
                attend(h - 1)
            attend(XA_HEADS - 1)
            pe.wait_ge(read["o"], 4)
            for i in range(4):
                dense(f"ao{i}", oT)
            pe.wait_ge(read["ao"], 4)
            pe.wait_ge(sem["wr_ready"], 1)
            ps = begin("rt0")
            for t in range(NT):
                for k in range(KD):
                    mm(ps[:, t * 64:t * 64 + NG + NE], xT[:, k, t * P:(t + 1) * P], wr[:, k, :],
                       start=k == 0, stop=k == KD - 1)
            pe.wait_ge(sem["x2sq_ready"], 4)
            for t in range(NT):
                for k in range(KD):
                    last = mm(ps[:, 128 + t:129 + t], x2sq[:, k, t * P:(t + 1) * P], ones[:, 0:1],
                              start=k == 0, stop=k == KD - 1)
            end(last)
            for i in range(4):
                to_N(f"tr{i}", i % 2, lambda f: xT[:, f, :], i // 2)
            pe.wait_ge(sem["assign_ready"], 1)
            asg = rt2("as")
            ps = begin("rk0")
            mm(ps[:, 0:NE], strict[:], asg[:, 0, :], start=True, stop=True)
            mm(ps[:, NE:2 * NE], ones[:], asg[:, 0, :], start=True, stop=False)
            mm(ps[:, NE:2 * NE], strict[:], asg[:, 1, :], start=False, stop=True)
            mm(ps[:, 2 * NE:3 * NE], ones[:], asg[:, 0, :], start=True, stop=False)
            end(mm(ps[:, 2 * NE:3 * NE], ones[:], asg[:, 1, :], start=False, stop=True))
            for name in order[RK - NB:RK]:
                pe.wait_ge(read[family(name)], member(name) + 1)
            for i in range(2 * NT):
                t, h = i // 2, i % 2
                mm(x3_bank[i][:, :], ident[:], x2N[:, t, h * 512:(h + 1) * 512], start=True, stop=False)
            pe.wait_ge(sem["h3_ready"], 1)
            for k in range(KD):
                ps = begin(f"ga{k}")
                for t in range(NT):
                    if k == 0:
                        pe.wait_ge(sem["sel_ready"], t + 1)
                    last = mm(ps[:, :], h3N[:, t, k * P:(k + 1) * P], sel[:, t, :], start=t == 0, stop=t == NT - 1)
                end(last)
            assert count[0] == len(order)
            pe.wait_ge(read["ga"], KD)

            def scatter(n, p, before=0):
                pe.wait_ge(sem["yS_ready"], n + (2 - before))
                for t in range(NT):
                    for h in range(2):
                        mm(x3_bank[2 * t + h][:, :], scat[h * WIN:(h + 1) * WIN, p, t * P:(t + 1) * P],
                           yS[h * WIN:(h + 1) * WIN, :], start=False, stop=False)

            def ffn(n, p, slots, xin, arrived, behind):
                pe.wait_ge(sem["xe_ready"], n + 1 + (xin != p))
                for j in range(2):
                    pe.wait_ge(filled[slots[j]], arrived(j))
                    w = slot(slots[j]).rearrange("p (k g n) -> p k g n", k=4, g=2)
                    for k in range(4):
                        for c in range(2):
                            last = mm(gu_bank(p)[c * WIN:(c + 1) * WIN, :], xe[:, xin, 4 * j + k, :],
                                      w[:, k, :, c * SEG:(c + 1) * SEG], start=4 * j + k == 0, stop=4 * j + k == KD - 1)
                    last.then_inc(sem["half_done" if j == 0 else "gu_done"], 1)
                    if j == 0:
                        pe.wait_ge(sem["placed_ready"], n + 1 + (xin != p))
                        for t in range(NT):
                            tp(turn_bank[:, T + t * P:T + (t + 1) * P],
                               placed[:, xin, t].rearrange("p d w -> p (d w)"), ident[:])
                if behind:
                    scatter(n, 1 - p, before=1)
                pe.wait_ge(sem["scat_ready"], n + 1)
                pe.wait_ge(sem["h_ready"], n + 1)
                for j in range(SEG // P):
                    last = tp(turn_bank[:, j * P:(j + 1) * P], hm[:, p, j * P:(j + 1) * P], ident[:])
                last.then_inc(sem["turn_done"], 1)
                pe.wait_ge(filled[slots[2]], arrived(2))
                pe.wait_ge(sem["hT_ready"], n + 1)
                w = slot(slots[2]).rearrange("p (k n) -> p k n", k=NF)
                for k in range(NF):
                    c, j = k // (SEG // P), k % (SEG // P)
                    for h in range(2):
                        last = mm(down_bank[h * WIN:(h + 1) * WIN, :], hmT[:, p, j, c * WIN:(c + 1) * WIN],
                                  w[:, k, h * 512:(h + 1) * 512], start=k == 0, stop=k == NF - 1)
                last.then_inc(sem["dn_done"], 1)

            with pe.Fori(0, NE // CYCLE) as i:
                for e in range(CYCLE):
                    slots = [(PARTS * e + j) % RING for j in range(PARTS)]

                    def arrived(j):
                        before = PREFILLS if slots[j] < PRE else 0
                        return (i * (PARTS * CYCLE // RING) + (before + (PARTS * e + j) // RING + 1)) * 16

                    ffn(i * CYCLE + e, e % 2, slots, e % 2, arrived, True)
            scatter(NE - 1, 1)
            pe.wait_ge(sem["ov_ready"], 1)
            n_ov = pe.value_load(ov_i[0:1, 0:1], min_val=0, max_val=NOV)
            with pe.If(n_ov > 0):
                with pe.Fori(0, n_ov) as o:
                    ffn(o + NE, 0, range(PARTS), 1, lambda j: (o + (PREFILLS + PARTS * NE // RING + 1)) * 16, False)
                    scatter(o + NE, 0)
            for i in range(2 * NT):
                mm(x3_bank[i][:, :].rearrange("p (a n) -> p a n", n=P), zeros[0:1, :],
                   zeros[0:1, :].rearrange("p (a n) -> p a n", a=1).to_broadcast([1, 512 // P, P]),
                   start=False, stop=True).then_inc(sem["x3_done"], 1)


_INS = ['x', 'mem', 'norm_mix', 'w_in', 'conv_a_w', 'conv_a_b', 'lru_gx_w', 'lru_gx_b', 'lru_ga_w',
        'lru_ga_b', 'lru_lambda', 'sgu_norm', 'sgu_w', 'sgu_b', 'conv_c_w', 'conv_c_b', 'ssm_dt_bias',
        'ssm_a_log', 'ssm_d', 'ssm_norm', 'w_a_proj', 'w_b_proj', 'w_c_proj', 'w_out', 'norm_xa',
        'norm_mem', 'w_q', 'w_kv', 'w_o', 'norm_ffn', 'w_router_group', 'b_router_group',
        'w_router_expert', 'b_router_expert', 'w_gate_up', 'w_down', 'norm_final']
_OUTS = [((1, 256, 1024), 'float32')]


def kernel(**inputs):
    import numpy as _np
    import concourse.bacc as _bacc
    from concourse import mybir as _mybir
    from concourse.bass_utils import run_bass_kernel_spmd as _run

    nc = _bacc.Bacc("TRN2", target_bir_lowering=False, num_devices=1)
    arrays, args = {}, []
    for name in _INS:
        a = _np.ascontiguousarray(inputs[name])
        arrays[f"in_{name}_dram"] = a
        args.append(nc.dram_tensor(f"in_{name}_dram", a.shape, _mybir.dt.from_np(a.dtype), kind="ExternalInput").ap())
    for i, (shape, dtype) in enumerate(_OUTS):
        dt = _mybir.dt.from_np(_np.dtype(dtype))
        args.append(nc.dram_tensor(f"out_{i}_dram", shape, dt, kind="ExternalOutput").ap())
    encoder_kernel(nc, *args)
    r = _run(nc, [arrays], core_ids=[0])
    return r.results[0]["out_0_dram"]
```
